# Optimizing a Trainium2 kernel written in Bass

```python
import jax, jax.numpy as jnp
from jax import lax
import numpy as np

D_MODEL = 1024
BATCH = 1
SEQ = 512
DEPTH = 2

N_A_LAYERS = DEPTH // 2
N_B_LAYERS = DEPTH - N_A_LAYERS
PLE_DIM = 256
NORM_EPS = 1e-6

DN_HEADS = 8
DN_DK = 128
DN_DV = 128
DN_CONV = 4
DN_CHUNK = 64
DN_QK = DN_HEADS * DN_DK
DN_V = DN_HEADS * DN_DV
DN_IN = 2 * DN_QK + 2 * DN_V + 2 * DN_HEADS

DIL_CONFIGS = ((128, 1), (512, 4), (2048, 16))
N_ATT_GROUPS = len(DIL_CONFIGS)
HEAD_DIM = 128
Q_PER_GROUP = 4
KV_PER_GROUP = 2
Q_REP = Q_PER_GROUP // KV_PER_GROUP
ATT_BLOCK = 128
ALIBI_MAX = 8.0
Q_WIDTH = N_ATT_GROUPS * Q_PER_GROUP * HEAD_DIM
KV_WIDTH = N_ATT_GROUPS * 2 * KV_PER_GROUP * HEAD_DIM
ATT_OUT = Q_PER_GROUP * HEAD_DIM

MOE_GROUPS = 4
MOE_EXPERTS_PER_GROUP = 8
MOE_EXPERTS = MOE_GROUPS * MOE_EXPERTS_PER_GROUP
MOE_TOPK = 2
MOE_HIDDEN = 512
MOE_BLOCK = 128

kernel_name = 'yoco_deltanet_dilated_hmoe'

def rms_norm(x, g):
    xf = x.astype(jnp.float32)
    y = xf * lax.rsqrt(jnp.mean(xf * xf, axis=-1, keepdims=True) + NORM_EPS)
    return (y * g.astype(jnp.float32)).astype(x.dtype)

def l2_norm(x):
    return x * lax.rsqrt(jnp.sum(x * x, axis=-1, keepdims=True) + NORM_EPS)

def alibi_slopes():
    n = N_ATT_GROUPS * Q_PER_GROUP
    s = 2.0 ** (-ALIBI_MAX * np.arange(1, n + 1) / n)
    return s.reshape(N_ATT_GROUPS, KV_PER_GROUP, Q_REP).astype(np.float32)

def causal_depthwise_conv(x, w):
    k, c = w.shape
    return lax.conv_general_dilated(x, w[:, None, :].astype(x.dtype), window_strides=(1,),
                                    padding=((k - 1, 0),), dimension_numbers=('NWC', 'WIO', 'NWC'),
                                    feature_group_count=c)

def _to_chunks(t, n_chunks):
    b, s, h = t.shape[:3]
    t = t.reshape((b, n_chunks, s // n_chunks, h) + t.shape[3:])
    return jnp.moveaxis(t, 3, 1)

def chunk_gated_delta_rule(q, k, v, beta, g_log):
    b, s, h, dk = q.shape
    dv = v.shape[-1]
    n = s // DN_CHUNK
    q, k, v = _to_chunks(q, n), _to_chunks(k, n), _to_chunks(v, n)
    beta, g = _to_chunks(beta, n), _to_chunks(g_log, n)
    g = jnp.cumsum(g, axis=-1)
    idx = jnp.arange(DN_CHUNK)
    causal = idx[:, None] >= idx[None, :]
    strict = idx[:, None] > idx[None, :]
    decay = jnp.exp(jnp.where(causal, g[..., :, None] - g[..., None, :], -jnp.inf))
    kk = jnp.einsum('bhnid,bhnjd->bhnij', k, k)
    a = jnp.where(strict, beta[..., :, None] * kk * decay, 0.0) + jnp.eye(DN_CHUNK, dtype=jnp.float32)
    rhs = jnp.concatenate([beta[..., None] * v, (beta * jnp.exp(g))[..., None] * k], axis=-1)
    sol = lax.linalg.triangular_solve(a, rhs, left_side=True, lower=True, unit_diagonal=True)
    u_t, w = sol[..., :dv], sol[..., dv:]
    attn = jnp.einsum('bhnid,bhnjd->bhnij', q, k) * decay
    q_g = q * jnp.exp(g)[..., None]
    g_last = g[..., -1]
    k_d = k * jnp.exp(g_last[..., None] - g)[..., None]

    def step(state, xs):
        u_tc, w_c, attn_c, qg_c, kd_c, gl_c = xs
        u = u_tc - jnp.einsum('bhcd,bhde->bhce', w_c, state)
        o = jnp.einsum('bhcd,bhde->bhce', qg_c, state) + jnp.einsum('bhij,bhje->bhie', attn_c, u)
        state = jnp.exp(gl_c)[..., None, None] * state + jnp.einsum('bhcd,bhce->bhde', kd_c, u)
        return state, o

    tr = lambda t: jnp.moveaxis(t, 2, 0)
    state0 = jnp.zeros((b, h, dk, dv), jnp.float32)
    _, o = lax.scan(step, state0, (tr(u_t), tr(w), tr(attn), tr(q_g), tr(k_d), tr(g_last)))
    return o.transpose(1, 0, 3, 2, 4).reshape(b, s, h, dv)

def gated_deltanet(xn, w_in, conv_w, a_log, dt_bias, o_norm, w_out):
    b, s, _ = xn.shape
    proj = xn @ w_in
    qkv = proj[..., :2 * DN_QK + DN_V]
    z = proj[..., 2 * DN_QK + DN_V:2 * DN_QK + 2 * DN_V]
    b_pre = proj[..., 2 * DN_QK + 2 * DN_V:2 * DN_QK + 2 * DN_V + DN_HEADS]
    a_pre = proj[..., 2 * DN_QK + 2 * DN_V + DN_HEADS:]
    qkv = jax.nn.silu(causal_depthwise_conv(qkv, conv_w))
    q = l2_norm(qkv[..., :DN_QK].reshape(b, s, DN_HEADS, DN_DK).astype(jnp.float32)) * (DN_DK ** -0.5)
    k = l2_norm(qkv[..., DN_QK:2 * DN_QK].reshape(b, s, DN_HEADS, DN_DK).astype(jnp.float32))
    v = qkv[..., 2 * DN_QK:].reshape(b, s, DN_HEADS, DN_DV).astype(jnp.float32)
    beta = jax.nn.sigmoid(b_pre.astype(jnp.float32))
    g_log = -jnp.exp(a_log.astype(jnp.float32)) * jax.nn.softplus(a_pre.astype(jnp.float32) + dt_bias.astype(jnp.float32))
    o = chunk_gated_delta_rule(q, k, v, beta, g_log)
    o = rms_norm(o, o_norm) * jax.nn.silu(z.reshape(b, s, DN_HEADS, DN_DV).astype(jnp.float32))
    return o.reshape(b, s, DN_V).astype(xn.dtype) @ w_out

def key_blocks(t, dil):
    b, s, hk, hd = t.shape
    l = s // dil
    nblk = -(-l // ATT_BLOCK)
    lp = nblk * ATT_BLOCK
    t = t.reshape(b, l, dil, hk, hd).transpose(0, 2, 3, 1, 4)
    t = jnp.pad(t, ((0, 0), (0, 0), (0, 0), (0, lp - l), (0, 0))).reshape(b, dil, hk, nblk, ATT_BLOCK, hd)
    prev = jnp.pad(t, ((0, 0), (0, 0), (0, 0), (1, 0), (0, 0), (0, 0)))[:, :, :, :-1]
    return jnp.concatenate([prev, t], axis=4)

def query_blocks(q, dil):
    b, s, hk, r, hd = q.shape
    l = s // dil
    nblk = -(-l // ATT_BLOCK)
    lp = nblk * ATT_BLOCK
    q = q.reshape(b, l, dil, hk, r, hd).transpose(0, 2, 3, 4, 1, 5)
    q = jnp.pad(q, ((0, 0), (0, 0), (0, 0), (0, 0), (0, lp - l), (0, 0)))
    return q.reshape(b, dil, hk, r, nblk, ATT_BLOCK, hd)

def dilated_branch(q, kb, vb, window, dil, slopes):
    b, s, hk, r, hd = q.shape
    l = s // dil
    nblk = kb.shape[3]
    lp = nblk * ATT_BLOCK
    qb = query_blocks(q, dil)
    sc = jnp.einsum('bdgrnqh,bdgnkh->bdgrnqk', qb, kb).astype(jnp.float32) * (hd ** -0.5)
    qi = jnp.arange(ATT_BLOCK)[:, None]
    ki = jnp.arange(2 * ATT_BLOCK)[None, :]
    dist = ATT_BLOCK + qi - ki
    key_pos = (jnp.arange(nblk) * ATT_BLOCK - ATT_BLOCK)[:, None, None] + ki[None]
    valid = (dist >= 0) & (dist <= window // dil) & (key_pos >= 0)
    bias = -jnp.asarray(slopes)[:, :, None, None, None] * (dil * dist).astype(jnp.float32)
    sc = jnp.where(valid, sc + bias, -jnp.inf)
    lse = jax.nn.logsumexp(sc, axis=-1)
    p = jnp.exp(sc - lse[..., None])
    o = jnp.einsum('bdgrnqk,bdgnkh->bdgrnqh', p.astype(vb.dtype), vb)
    o = o.reshape(b, dil, hk, r, lp, hd)[:, :, :, :, :l].transpose(0, 4, 1, 2, 3, 5).reshape(b, s, hk * r, hd)
    lse = lse.reshape(b, dil, hk, r, lp)[..., :l].transpose(0, 4, 1, 2, 3).reshape(b, s, hk * r)
    return o, lse

def shared_dilated_kv(h, kv_norm, w_kv, k_norm):
    b, s, _ = h.shape
    kv = (rms_norm(h, kv_norm) @ w_kv).reshape(b, s, N_ATT_GROUPS, 2, KV_PER_GROUP, HEAD_DIM)
    blocks = []
    for g, (window, dil) in enumerate(DIL_CONFIGS):
        k = rms_norm(kv[:, :, g, 0], k_norm[g])
        v = kv[:, :, g, 1]
        blocks.append((key_blocks(k, dil), key_blocks(v, dil)))
    return blocks

def dilated_attention(xn, w_q, q_norm, w_out, kv_blocks):
    b, s, _ = xn.shape
    q = (xn @ w_q).reshape(b, s, N_ATT_GROUPS, KV_PER_GROUP, Q_REP, HEAD_DIM)
    slopes = alibi_slopes()
    outs, lses = [], []
    for g, (window, dil) in enumerate(DIL_CONFIGS):
        qg = rms_norm(q[:, :, g], q_norm[g])
        o, lse = dilated_branch(qg, kv_blocks[g][0], kv_blocks[g][1], window, dil, slopes[g])
        outs.append(o)
        lses.append(lse)
    o = jnp.stack(outs).astype(jnp.float32)
    wts = jax.nn.softmax(jnp.stack(lses), axis=0)
    o = jnp.sum(wts[..., None] * o, axis=0)
    return o.reshape(b, s, ATT_OUT).astype(xn.dtype) @ w_out

def grouped_expert_mlp(xt, eid, ew, w1, w3, w2):
    n_tok, d = xt.shape
    n_exp = w1.shape[0]
    flat_e = eid.reshape(-1)
    flat_t = jnp.arange(flat_e.shape[0]) // eid.shape[1]
    flat_w = ew.reshape(-1)
    m = flat_e.shape[0]
    order = jnp.argsort(flat_e)
    se, st, sw = flat_e[order], flat_t[order], flat_w[order]
    counts = jnp.bincount(flat_e, length=n_exp)
    starts = jnp.cumsum(counts) - counts
    padded = (counts + MOE_BLOCK - 1) // MOE_BLOCK * MOE_BLOCK
    pad_ends = jnp.cumsum(padded)
    pad_starts = pad_ends - padded
    dest = pad_starts[se] + jnp.arange(m) - starts[se]
    n_blocks = -(-m // MOE_BLOCK) + n_exp
    rows = n_blocks * MOE_BLOCK
    row_tok = jnp.full((rows,), n_tok, jnp.int32).at[dest].set(st.astype(jnp.int32))
    row_w = jnp.zeros((rows,), jnp.float32).at[dest].set(sw)
    block_e = jnp.minimum(jnp.searchsorted(pad_ends, jnp.arange(n_blocks) * MOE_BLOCK, side='right'), n_exp - 1)
    x_rows = jnp.concatenate([xt, jnp.zeros((1, d), xt.dtype)])[row_tok].reshape(n_blocks, MOE_BLOCK, d)

    def block_mlp(args):
        xb, e = args
        hdn = jax.nn.silu(xb @ w1[e]) * (xb @ w3[e])
        return hdn @ w2[e]

    y = lax.map(block_mlp, (x_rows, block_e)).reshape(rows, d)
    out = jnp.zeros((n_tok + 1, d), y.dtype).at[row_tok].add(y * row_w[:, None].astype(y.dtype))
    return out[:n_tok]

def hierarchical_moe(xn, w_rg, b_rg, w_re, b_re, w1, w3, w2):
    b, s, d = xn.shape
    xt = xn.reshape(-1, d)
    n = xt.shape[0]
    xf = xt.astype(jnp.float32)
    gp = jax.nn.softmax(xf @ w_rg.astype(jnp.float32) + b_rg.astype(jnp.float32), axis=-1)
    g_idx = jnp.argmax(gp, axis=-1)
    g_w = jnp.take_along_axis(gp, g_idx[:, None], axis=-1)
    el = (xf @ w_re.astype(jnp.float32) + b_re.astype(jnp.float32)).reshape(n, MOE_GROUPS, MOE_EXPERTS_PER_GROUP)
    el = jnp.take_along_axis(el, g_idx[:, None, None], axis=1)[:, 0]
    top_p, top_i = lax.top_k(jax.nn.softmax(el, axis=-1), MOE_TOPK)
    wts = g_w * top_p / jnp.sum(top_p, axis=-1, keepdims=True)
    eid = g_idx[:, None] * MOE_EXPERTS_PER_GROUP + top_i
    return grouped_expert_mlp(xt, eid, wts, w1, w3, w2).reshape(b, s, d)

def per_layer_embedding(h, p_i, g_norm, w_gate, w_proj):
    gate = jax.nn.sigmoid((rms_norm(h, g_norm) @ w_gate).astype(jnp.float32))
    return (gate * (p_i @ w_proj).astype(jnp.float32)).astype(h.dtype)

def setup_inputs(seed: int = 0) -> dict:
    key = jax.random.key(seed)
    ks = jax.random.split(key, 32)
    f32 = jnp.float32
    nrm = lambda k, shape, sc: jax.random.normal(k, shape, f32) * sc
    gain = lambda k, shape: 1.0 + 0.05 * jax.random.normal(k, shape, f32)
    dt = jnp.exp(jax.random.uniform(ks[5], (N_A_LAYERS, DN_HEADS), f32, np.log(1e-3), np.log(1e-1)))
    return {
        'x': nrm(ks[0], (BATCH, SEQ, D_MODEL), 1.0),
        'p': nrm(ks[1], (DEPTH, BATCH, SEQ, PLE_DIM), 1.0),
        'a_norm': gain(ks[2], (N_A_LAYERS, D_MODEL)),
        'a_w_in': nrm(ks[3], (N_A_LAYERS, D_MODEL, DN_IN), D_MODEL ** -0.5),
        'a_conv': nrm(ks[4], (N_A_LAYERS, DN_CONV, 2 * DN_QK + DN_V), DN_CONV ** -0.5),
        'a_A_log': jnp.log(jax.random.uniform(ks[6], (N_A_LAYERS, DN_HEADS), f32, 1.0, 16.0)),
        'a_dt_bias': dt + jnp.log(-jnp.expm1(-dt)),
        'a_o_norm': gain(ks[7], (N_A_LAYERS, DN_DV)),
        'a_w_out': nrm(ks[8], (N_A_LAYERS, DN_V, D_MODEL), DN_V ** -0.5),
        'kv_norm': gain(ks[9], (D_MODEL,)),
        'w_kv': nrm(ks[10], (D_MODEL, KV_WIDTH), D_MODEL ** -0.5),
        'k_norm': gain(ks[11], (N_ATT_GROUPS, HEAD_DIM)),
        'b_norm': gain(ks[12], (N_B_LAYERS, D_MODEL)),
        'b_w_q': nrm(ks[13], (N_B_LAYERS, D_MODEL, Q_WIDTH), D_MODEL ** -0.5),
        'b_q_norm': gain(ks[14], (N_B_LAYERS, N_ATT_GROUPS, HEAD_DIM)),
        'b_w_out': nrm(ks[15], (N_B_LAYERS, ATT_OUT, D_MODEL), ATT_OUT ** -0.5),
        'ffn_norm': gain(ks[16], (DEPTH, D_MODEL)),
        'w_router_group': nrm(ks[17], (DEPTH, D_MODEL, MOE_GROUPS), D_MODEL ** -0.5),
        'b_router_group': nrm(ks[18], (DEPTH, MOE_GROUPS), 0.01),
        'w_router_expert': nrm(ks[19], (DEPTH, D_MODEL, MOE_EXPERTS), D_MODEL ** -0.5),
        'b_router_expert': nrm(ks[20], (DEPTH, MOE_EXPERTS), 0.01),
        'w1': nrm(ks[21], (DEPTH, MOE_EXPERTS, D_MODEL, MOE_HIDDEN), D_MODEL ** -0.5),
        'w3': nrm(ks[22], (DEPTH, MOE_EXPERTS, D_MODEL, MOE_HIDDEN), D_MODEL ** -0.5),
        'w2': nrm(ks[23], (DEPTH, MOE_EXPERTS, MOE_HIDDEN, D_MODEL), MOE_HIDDEN ** -0.5),
        'ple_norm': gain(ks[24], (DEPTH, D_MODEL)),
        'w_ple_gate': nrm(ks[25], (DEPTH, D_MODEL, D_MODEL), D_MODEL ** -0.5),
        'w_ple_proj': nrm(ks[26], (DEPTH, PLE_DIM, D_MODEL), PLE_DIM ** -0.5),
    }

def reference(x, p, a_norm, a_w_in, a_conv, a_A_log, a_dt_bias, a_o_norm, a_w_out,
              kv_norm, w_kv, k_norm, b_norm, b_w_q, b_q_norm, b_w_out,
              ffn_norm, w_router_group, b_router_group, w_router_expert, b_router_expert,
              w1, w3, w2, ple_norm, w_ple_gate, w_ple_proj):
    h = x
    kv_blocks = None
    for i in range(DEPTH):
        if i < N_A_LAYERS:
            a = i
            h = h + gated_deltanet(rms_norm(h, a_norm[a]), a_w_in[a], a_conv[a], a_A_log[a],
                                   a_dt_bias[a], a_o_norm[a], a_w_out[a])
        else:
            bl = i - N_A_LAYERS
            h = h + dilated_attention(rms_norm(h, b_norm[bl]), b_w_q[bl], b_q_norm[bl], b_w_out[bl], kv_blocks)
        h = h + hierarchical_moe(rms_norm(h, ffn_norm[i]), w_router_group[i], b_router_group[i],
                                 w_router_expert[i], b_router_expert[i], w1[i], w3[i], w2[i])
        h = h + per_layer_embedding(h, p[i], ple_norm[i], w_ple_gate[i], w_ple_proj[i])
        if i == N_A_LAYERS - 1:
            kv_blocks = shared_dilated_kv(h, kv_norm, w_kv, k_norm)
    return h


_drawn_inputs = setup_inputs


def setup_inputs(seed=0):
    import zlib

    import numpy as np

    out = dict(_drawn_inputs(seed))
    spreads = {}
    factors = {'k_norm': 3.583,
     'b_norm': 2.94,
     'b_q_norm': 3.031,
     'b_router_group': 3.682,
     'b_router_expert': 4.455,
     'ple_norm': 3.539}
    for name, (base, spread) in spreads.items():
        noise = np.random.default_rng([zlib.crc32(name.encode()), seed]).standard_normal(out[name].shape)
        drawn = base * np.exp(spread * noise) if base else spread * noise
        out[name] = __import__('jax').numpy.asarray(drawn.astype(out[name].dtype))
    for name, factor in factors.items():
        out[name] = (out[name] * factor).astype(out[name].dtype)
    return out
```

```python
from contextlib import ExitStack

import concourse.bass as bass
from concourse import mybir
import numpy as np

F32 = mybir.dt.float32
BF16 = mybir.dt.bfloat16
I32 = mybir.dt.int32
ACT = mybir.ActivationFunctionType
ALU = mybir.AluOpType
AX = mybir.AxisListType

P = 128
D = 1024
SEQ = 512
NT = SEQ // P
DC = D // P
HALF = 512
EPS = 1e-6
PLE = 256
HEADS, DK = 8, 128
CONV = 4
QKV = 3 * HEADS * DK
GROUPS, QPG, KVPG, HD = 3, 4, 2, 128
DILS, WINDOW = (1, 4, 16), 128
MG, ME = 4, 8
EXPERTS = MG * ME
PAIRS = EXPERTS // 2
FF = 512
FC = FF // P
SLOTS = 64
BIG = 1e30
NOT_CHOSEN = 65536.0
RING = 6


def wait(eng, sem, value):
    if isinstance(value, int) and value <= 0:
        return
    eng.wait_ge(sem, value)


class Chain:

    def __init__(self, eng, sem, start=0):
        self.eng, self.sem, self.n, self.start = eng, sem, 0, start

    def link(self, ins):
        self.n += 1
        ins.then_inc(self.sem, 1)
        self.eng.wait_ge(self.sem, self.start + self.n)


class Ring:

    def __init__(self, buf, landed):
        self.buf, self.landed = buf, landed
        self.free, self.takes = [None] * RING, [0] * RING

    def load(self, sp, slot, dst, src):
        if self.free[slot]:
            sp.wait_ge(*self.free[slot])
        sp.dma_start(dst, src).then_inc(self.landed[slot], 16)

    def arrived(self, pe, slot, i=0):
        pe.wait_ge(self.landed[slot], (self.takes[slot] + 1 + i) * 16)

    def taken(self, slot, sem, value):
        self.takes[slot] += 1
        self.free[slot] = (sem, value)

    def flat(self, slot, n=4096):
        return self.buf[:, slot, 0:n]


class Net:
    pass


def bcast(ap, axis, n):
    shape = list(ap.shape)
    shape.insert(axis, n)
    return ap.unsqueeze(axis).to_broadcast(shape)




def load_expert_pair(k, layer, pair, load):
    for m, (w, chunks) in enumerate(((k.w1, DC), (k.w3, DC), (k.w2, FC))):
        src = w[layer].rearrange("(q e) (p c) n -> q p e (c n)", e=2, c=chunks)
        for half in range(2):
            slot = 2 * m + half
            load(slot, k.ring[:, slot, :].rearrange("p (e x) -> p e x", e=2),
                 src[bass.ds(pair, 1), :, :, half * 2048:(half + 1) * 2048].rearrange("q p e x -> (q p) e x"))


def prefetch_experts(sp, k, layer, slots=range(RING)):
    load_expert_pair(k, layer, 0, lambda slot, dst, src: k.R.load(sp, slot, dst, src) if slot in slots else None)


def prefetch_ple(sp, k, layer):
    src = k.w_gate[layer].rearrange("(p c) n -> p c n", c=DC)
    for half in range(2):
        k.R.load(sp, half, k.R.flat(half).rearrange("p (c n) -> p c n", c=DC),
                 src[:, :, half * HALF:(half + 1) * HALF])
    k.R.load(sp, 2, k.R.flat(2, 2048), k.w_proj[layer].rearrange("(p c) n -> p (c n)", c=2))




def norm_semaphores(k, tag):
    s = Net()
    (s.ss, s.var, s.std, s.rstd, s.xn, s.xn_odd, s.turned, s.xnT, s.xnT_odd) = (
        k.sem(f"{tag}_{name}") for name in
        ("ss", "var", "std", "rstd", "xn", "xn_odd", "turned", "xnT", "xnT_odd"))
    return s


def norm_chunk(pe, s, c):
    pe.wait_ge(s.xnT_odd if c % 2 else s.xnT, c // 2 + 1)


def norm_scalar(act, k, s, gain, fresh=True, meanwhile=None):
    if fresh:
        norm_scalar_rows(act, k, s)
    if meanwhile:
        meanwhile()
    for c in range(1, DC, 2):
        act.wait_ge(s.turned, c + 1)
        act.activation(k.xnT[:, c, :], k.bank[c][:, :], ACT.Copy, scale=gain[:, c:c + 1]).then_inc(s.xnT_odd, 1)


def norm_scalar_rows(act, k, s):
    for t in range(NT):
        act.activation(k.xn[:, t, :], k.H[:, t, :], ACT.Square, accum_out=k.ss[:, t:t + 1]).then_inc(s.ss, 1)
    act.wait_ge(s.var, 1)
    act.activation(k.std[:, :], k.var[:, :], ACT.Sqrt).then_inc(s.std, 1)
    act.wait_ge(s.rstd, 1)
    for t in range(1, NT, 2):
        act.activation(k.xn[:, t, :], k.H[:, t, :], ACT.Copy, scale=k.rstd[:, t:t + 1]).then_inc(s.xn_odd, 1)


def norm_vector(dve, k, s, gain, fresh=True):
    if fresh:
        norm_vector_rows(dve, k, s)
    for c in range(0, DC, 2):
        dve.wait_ge(s.turned, c + 1)
        dve.tensor_scalar(k.xnT[:, c, :], k.bank[c][:, :], gain[:, c:c + 1], None, ALU.mult).then_inc(s.xnT, 1)


def norm_vector_rows(dve, k, s):
    dve.wait_ge(s.ss, NT)
    dve.tensor_scalar(k.var[:, :], k.ss[:, :], 1.0 / D, EPS, ALU.mult, ALU.add).then_inc(s.var, 1)
    dve.wait_ge(s.std, 1)
    dve.reciprocal(k.rstd[:, :], k.std[:, :]).then_inc(s.rstd, 1)
    dve.wait_ge(s.rstd, 1)
    for t in range(0, NT, 2):
        dve.tensor_scalar(k.xn[:, t, :], k.H[:, t, :], k.rstd[:, t:t + 1], None, ALU.mult).then_inc(s.xn, 1)


def norm_tensor(pe, k, s, fresh=True):
    for t in range(NT):
        if fresh:
            pe.wait_ge(s.xn_odd if t % 2 else s.xn, t // 2 + 1)
        for c in range(DC):
            last = pe.transpose(k.bank[c][:, t * P:(t + 1) * P], k.xn[:, t, c::DC], k.ident)
            if t == NT - 1:
                last.then_inc(s.turned, 1)




def delta_gates(k, following):
    s = norm_semaphores(k, "dg")
    (s.loads, s.ab, s.eb, s.shifted, s.es, s.ln, s.eA, s.glog, s.sums, s.eG, s.diff, s.steps, s.acts) = (
        k.sem(f"dg_{name}") for name in
        ("loads", "ab", "eb", "shifted", "es", "ln", "eA", "glog", "sums", "eG", "diff", "steps", "acts"))
    gain = k.g_a
    with nc_block(k) as block:

        @block.tensor
        def _(pe):
            norm_tensor(pe, k, s)
            pe.wait_ge(s.loads, 16)
            norm_chunk(pe, s, DC - 2)
            norm_chunk(pe, s, DC - 1)
            for t in range(NT):
                for c in range(DC):
                    last = pe.matmul(k.bank[0][:, t * 2 * HEADS:(t + 1) * 2 * HEADS], k.xnT[:, c, t * P:(t + 1) * P],
                                     k.w_ab[:, c, :], start=(c == 0), stop=(c == DC - 1))
            last.then_inc(s.ab, 1)
            pe.wait_ge(s.glog, 1)
            g = k.glog[:, :, :].rearrange("p t h -> p (t h)")
            pe.matmul(k.bank[1][:, 0:NT * HEADS], k.upto, g, start=True, stop=True)
            pe.matmul(k.bank[1][:, NT * HEADS:2 * NT * HEADS], k.ones, g, start=True, stop=True).then_inc(s.sums, 1)

        @block.scalar
        def _(act):
            norm_scalar(act, k, s, gain)
            ab = k.bank[0][:, 0:NT * 2 * HEADS].rearrange("p (t h) -> p t h", t=NT)
            act.wait_ge(s.shifted, 1)
            act.activation(k.beta[:, :, :], ab[:, :, 0:HEADS], ACT.Exp, scale=-1.0).then_inc(s.eb, 1)
            act.activation(k.eA[:, :], k.eA[:, :], ACT.Exp).then_inc(s.eA, 1)
            act.activation(k.sp[:, :, :], k.sp[:, :, :], ACT.Exp, scale=-1.0).then_inc(s.es, 1)
            act.wait_ge(s.es, 1)
            act.activation(k.sp[:, :, :], k.sp[:, :, :], ACT.Ln, bias=1.0).then_inc(s.ln, 1)
            act.wait_ge(s.sums, 1)
            act.activation(k.eG[:, :, :].rearrange("p t h -> p (t h)"), k.bank[1][:, 0:NT * HEADS],
                           ACT.Exp).then_inc(s.eG, 1)
            act.activation(k.eGlast[:, :, :].rearrange("p t h -> p (t h)"), k.bank[1][:, NT * HEADS:2 * NT * HEADS],
                           ACT.Exp).then_inc(s.acts, 1)
            act.wait_ge(s.diff, 1)
            act.activation(k.eGrest[:, :, :], k.eGrest[:, :, :], ACT.Exp).then_inc(s.acts, 1)

        @block.vector
        def _(dve):
            norm_vector(dve, k, s, gain)
            ch = Chain(dve, s.steps)
            ab = k.bank[0][:, 0:NT * 2 * HEADS].rearrange("p (t h) -> p t h", t=NT)
            dve.wait_ge(s.ab, 1)
            ch.link(dve.tensor_tensor(k.ax[:, :, :], ab[:, :, HEADS:], bcast(k.dt_bias[:, :], 1, NT), ALU.add))
            ch.link(dve.tensor_scalar(k.sp[:, :, :], k.ax[:, :, :], -1.0, None, ALU.mult))
            dve.tensor_tensor(k.sp[:, :, :], k.sp[:, :, :], k.ax[:, :, :], ALU.max).then_inc(s.shifted, 1)
            dve.wait_ge(s.eb, 1)
            ch.link(dve.tensor_scalar(k.beta[:, :, :], k.beta[:, :, :], 1.0, None, ALU.add))
            ch.link(dve.reciprocal(k.beta[:, :, :], k.beta[:, :, :]))
            dve.wait_ge(s.ln, 1)
            ch.link(dve.scalar_tensor_tensor(k.ax[:, :, :], k.ax[:, :, :], 0.0, k.sp[:, :, :], ALU.max, ALU.add))
            dve.wait_ge(s.eA, 1)
            dve.scalar_tensor_tensor(k.glog[:, :, :], k.ax[:, :, :], -1.0, bcast(k.eA[:, :], 1, NT), ALU.mult,
                                     ALU.mult).then_inc(s.glog, 1)
            dve.wait_ge(s.acts, 1)
            G = k.G[:, :, :].rearrange("p t h -> p (t h)")
            ch.link(dve.tensor_copy(G, k.bank[1][:, 0:NT * HEADS]))
            dve.tensor_tensor(k.eGrest[:, :, :].rearrange("p t h -> p (t h)"),
                              k.bank[1][:, NT * HEADS:2 * NT * HEADS], G, ALU.subtract).then_inc(s.diff, 1)
            dve.tensor_tensor(k.beG[:, :, :], k.beta[:, :, :], k.eG[:, :, :], ALU.mult).then_inc(s.steps, 1)

        @block.sync
        def _(sp):
            sp.dma_start(k.w_ab[:, :, :], k.w_ab_d.rearrange("(p c) n -> p c n", c=DC)).then_inc(s.loads, 16)
            following(sp)


def load_head(k, h, slot):
    return k.ring[:, slot, :], k.w_heads[bass.ds(h, 1), :, :].rearrange("h p x -> (h p) x")


def head_of(ap, h):
    return ap[:, :, bass.ds(h, 1)].rearrange("p t h -> p (t h)")


LEVELS = P.bit_length() - 1


def delta_heads(k, following):
    s = Net()
    (s.proj, s.ssq, s.grams, s.turned, s.Vt, s.X, s.Y, s.Z, s.W, s.u, s.o, s.dS, s.oss, s.sil, s.sq, s.ln,
     s.rn, s.dec, s.eg, s.Xs, s.V0, s.nW, s.us, s.osq, s.conv, s.cstep, s.qkn, s.gB, s.clip, s.L, s.A, s.T0,
     s.Vs, s.Ts, s.v_turned, s.tok, s.qg, s.St, s.og, s.vstep, s.C) = (
        k.sem(f"dn_{name}") for name in (
            "proj", "ssq", "grams", "turned", "Vt", "X", "Y", "Z", "W", "u", "o", "dS", "oss", "sil", "sq",
            "ln", "rn", "dec", "eg", "Xs", "V0", "nW", "us", "osq", "conv", "cstep", "qkn", "gB", "clip",
            "L", "A", "T0", "Vs", "Ts", "v_turned", "tok", "qg", "St", "og", "vstep", "C"))
    R = k.R
    bank = k.bank
    nl = LEVELS - 1
    tile = lambda a, t: a[:, t * P:(t + 1) * P]
    four = lambda a: a.rearrange("p (t n) -> p t n", t=NT)

    def blocks(a, l, odd):
        if len(a.shape) == 3:
            a = a.rearrange("p t n -> p (t n)")
        return a.rearrange("p (n two b) -> p n two b", two=2, b=1 << l)[:, :, odd, :]

    with nc_block(k) as block:

        @block.tensor
        def _(pe):
            def projection(h, par):
                pe.wait_ge(R.landed[par], h * 8 + (16 * (R.takes[par] + 1) - 8 * par))
                w = R.flat(par).rearrange("p (c j n) -> p c j n", c=DC, j=4)
                for j in range(4):
                    if j == 0:
                        wait(pe, s.conv, 3 * h)
                    elif j == 1:
                        wait(pe, s.sil, 4 * h)
                    else:
                        pe.wait_ge(s.conv, 3 * h + j - 1)
                    for c in range(DC):
                        m = pe.matmul(bank[j % 2][:, :], w[:, c, j, :], k.xnT[:, c, :], start=(c == 0),
                                      stop=(c == DC - 1))
                        if c == DC - 1:
                            m.then_inc(s.proj, 1)
                        yield

            def norm_sums(h, j, par):
                pe.wait_ge(s.sq, 2 * h + j + 1)
                pe.matmul(bank[(2, 5)[j]][:, :], k.ones, k.sqr[:, j, :], start=True, stop=True).then_inc(s.ssq, 1)

            def head(h, par, follow=True):
                q, kk, v = (k.qkvz[:, par, j, :] for j in range(3))
                rest = projection(h + 1, 1 - par) if follow else iter(())

                def gap(n):
                    for _ in range(n):
                        next(rest, None)

                pe.wait_ge(s.qkn, 2 * h + 2)
                pe.wait_ge(s.gB, h + 1)
                for t in range(NT):
                    pe.matmul(tile(bank[5], t), k.glogB[:, t, :], k.upto, start=True, stop=True)
                for t in range(NT):
                    pe.matmul(tile(bank[3], t), tile(kk, t), tile(kk, t), start=True, stop=True)
                for t in range(NT):
                    last = pe.matmul(tile(bank[4], t), tile(kk, t), tile(q, t), start=True, stop=True)
                last.then_inc(s.grams, 1)
                for t in range(NT):
                    last = pe.transpose(tile(bank[6], t), tile(kk, t), k.ident)
                last.then_inc(s.turned, 1)
                gap(6)
                pe.wait_ge(s.T0, h + 1)
                for t in range(NT):
                    last = pe.transpose(tile(bank[3], t), k.T[:, t, :], k.ident)
                last.then_inc(s.Vt, 1)
                gap(1)
                for l in range(1, LEVELS):
                    pe.wait_ge(s.C, nl * h + l)
                    if l == 1:
                        pe.wait_ge(s.V0, h + 1)
                    else:
                        pe.wait_ge(s.Vs, nl * h + l - 1)
                    for t in range(NT):
                        last = pe.matmul(tile(bank[3], t), k.C[:, l, t, :], k.V[:, t, :], start=True, stop=True)
                    last.then_inc(s.X, 1)
                    gap(1)
                    pe.wait_ge(s.Xs, nl * h + l)
                    if l == 1:
                        pe.wait_ge(s.A, h + 1)
                        pe.wait_ge(s.eg, h + 1)
                    else:
                        pe.wait_ge(s.Ts, (nl - 1) * h + l - 1)
                    for t in range(NT):
                        last = pe.matmul(tile(bank[4], t), k.T[:, t, :], k.X[:, t, :], start=True, stop=True)
                    last.then_inc(s.Y, 1)
                    if l < nl:
                        for t in range(NT):
                            last = pe.matmul(tile(bank[5], t), k.X[:, t, :], k.T[:, t, :], start=True, stop=True)
                        last.then_inc(s.Z, 1)
                    gap(1)
                    if l == 2:
                        pe.wait_ge(s.sil, 4 * h + 3)
                        wait(pe, s.og, h)
                        for t in range(NT):
                            last = pe.transpose(tile(bank[7], t), tile(v, t), k.ident)
                        last.then_inc(s.v_turned, 1)
                pe.wait_ge(s.tok, 3 * h + 3)
                pe.wait_ge(s.Vs, nl * h + nl)
                for t in range(NT):
                    last = pe.matmul(tile(bank[6], t), k.kb[:, t, :], k.V[:, t, :], start=True, stop=True)
                last.then_inc(s.W, 1)
                if follow:
                    norm_sums(h + 1, 0, 1 - par)
                    pe.wait_ge(s.Ts, (nl - 1) * (h + 1))
                    norm_sums(h + 1, 1, 1 - par)
                for t in range(NT):
                    last = pe.matmul(tile(bank[3], t), k.V[:, t, :], k.vb[:, t, :], start=True, stop=(t == 0),
                                     skip_group_check=True)
                    if t:
                        pe.wait_ge(s.nW, h + 1)
                        pe.wait_ge(s.St, 3 * h + t)
                        last = pe.matmul(tile(bank[3], t), tile(k.nWT[:, :], t), k.state[:, (t - 1) % 2, :],
                                         start=False, stop=True, skip_group_check=True)
                    last.then_inc(s.u, 1)
                    gap(1)
                    pe.wait_ge(s.us, 4 * h + t + 1)
                    if t < NT - 1:
                        pe.matmul(tile(bank[4], t), k.kd[:, t, :], k.us[:, t, :], start=True,
                                  stop=True).then_inc(s.dS, 1)
                    if t == 0:
                        pe.wait_ge(s.qg, h + 1)
                        pe.wait_ge(s.A, h + 1)
                    else:
                        pe.matmul(tile(bank[7], t), k.state[:, (t - 1) % 2, :], tile(k.qg[:, :], t), start=True,
                                  stop=False, skip_group_check=True)
                    last = pe.matmul(tile(bank[7], t), k.us[:, t, :], k.A[:, t, :], start=(t == 0), stop=True,
                                     skip_group_check=True)
                    if t == NT - 1:
                        last.then_inc(s.o, 1)
                    gap(1)
                gap(1)
                pe.wait_ge(s.osq, h + 1)
                pe.matmul(bank[4][:, :], k.ones, k.osq[:, :], start=True, stop=True).then_inc(s.oss, 1)
                gap(32)

            for _ in projection(0, 0):
                pass
            norm_sums(0, 0, 0)
            norm_sums(0, 1, 0)
            head(0, 0)
            head(1, 1)
            with pe.Fori(1, HEADS // 2 - 1) as i:
                head(2 * i, 0)
                head(2 * i + 1, 1)
            head(HEADS - 2, 0)
            head(HEADS - 1, 1, follow=False)
            for slot in range(2):
                R.takes[slot] += HEADS // 2
                R.free[slot] = (s.proj, 4 * HEADS)

        @block.vector
        def _(dve):
            def conv(h, j, par):
                x, out = bank[j % 2], k.cv[:, j, :]
                tap = lambda n: k.conv_w[:, j, bass.ds(h * CONV + n, 1)]
                dve.wait_ge(s.proj, 4 * h + j + 1)
                base = 9 * h + 3 * j
                dve.tensor_scalar(out, x[:, :], tap(CONV - 1), None, ALU.mult).then_inc(s.cstep, 1)
                for n in range(1, CONV):
                    dve.wait_ge(s.cstep, base + n)
                    ins = dve.scalar_tensor_tensor(out[:, n:], x[:, 0:SEQ - n], tap(CONV - 1 - n), out[:, n:],
                                                   ALU.mult, ALU.add)
                    ins.then_inc(s.conv if n == CONV - 1 else s.cstep, 1)

            def normalise(h, j, par):
                dve.wait_ge(s.rn, j + 1 if isinstance(h, int) and h == 0 else 3 * h + j)
                a = k.qkvz[:, par, j, :]
                if j == 0:
                    dve.scalar_tensor_tensor(a, a, DK ** -0.5, k.rnorm[:, 0, :], ALU.mult,
                                             ALU.mult).then_inc(s.qkn, 1)
                else:
                    dve.tensor_tensor(a, a, k.rnorm[:, 1, :], ALU.mult).then_inc(s.qkn, 1)

            def decays(h):
                dve.tensor_copy(k.glogB[:, :, :], bcast(head_of(k.glog, h), 2, P)).then_inc(s.gB, 1)

            def head(h, par, follow=True):
                q = k.qkvz[:, par, 0, :]
                n = 0
                vbase = VSTEPS * h

                def link(ins):
                    nonlocal n
                    n += 1
                    ins.then_inc(s.vstep, 1)
                    dve.wait_ge(s.vstep, vbase + n)

                dve.wait_ge(s.grams, h + 1)
                link(dve.tensor_tensor(k.dif[:, :, :], four(bank[5][:, :]), bcast(head_of(k.G, h), 2, P),
                                       ALU.subtract))
                dve.tensor_scalar(k.lo[:, :, :], k.dif[:, :, :], 0.0, None, ALU.max).then_inc(s.clip, 1)
                dve.tensor_scalar(k.hi[:, :, :], k.dif[:, :, :], 0.0, None, ALU.min).then_inc(s.clip, 1)
                dve.wait_ge(s.turned, h + 1)
                dve.tensor_tensor(k.kb[:, :, :], four(bank[6][:, :]), bcast(head_of(k.beG, h), 2, P),
                                  ALU.mult).then_inc(s.tok, 1)
                dve.wait_ge(s.dec, 2 * h + 1)
                link(dve.tensor_tensor(k.lo[:, :, :], k.lo[:, :, :], four(bank[3][:, :]), ALU.mult))
                dve.tensor_tensor(k.lo[:, :, :], k.lo[:, :, :], bcast(head_of(k.beta, h), 2, P),
                                  ALU.mult).then_inc(s.L, 1)
                dve.wait_ge(s.L, h + 1)
                link(dve.tensor_tensor(k.C[:, 0, :, :], k.lo[:, :, :], bcast(k.join[:, 0, :], 1, NT), ALU.mult))
                dve.scalar_tensor_tensor(k.T[:, :, :], k.C[:, 0, :, :], -1.0, bcast(k.ident, 1, NT), ALU.mult,
                                         ALU.add).then_inc(s.T0, 1)
                dve.wait_ge(s.dec, 2 * h + 2)
                link(dve.tensor_tensor(k.A[:, :, :], k.hi[:, :, :], four(bank[4][:, :]), ALU.mult))
                dve.tensor_tensor(k.A[:, :, :], k.A[:, :, :], bcast(k.upto, 1, NT), ALU.mult).then_inc(s.A, 1)
                dve.tensor_tensor(k.kd[:, :, :], four(bank[6][:, :]), bcast(head_of(k.eGrest, h), 2, P),
                                  ALU.mult).then_inc(s.tok, 1)
                dve.wait_ge(s.eg, h + 1)
                dve.tensor_tensor(k.qg[:, :], q, k.eGrow[:, :], ALU.mult).then_inc(s.qg, 1)
                for l in range(1, LEVELS):
                    dve.wait_ge(s.Y, nl * h + l)
                    if l > 1:
                        dve.wait_ge(s.Vs, nl * h + l - 1)
                    V = blocks(k.V[:, :, :], l, 1)
                    dve.tensor_tensor(V, V, blocks(bank[4], l, 1), ALU.subtract).then_inc(s.Vs, 1)
                    if l < nl:
                        dve.wait_ge(s.Z, (nl - 1) * h + l)
                        dve.wait_ge(s.Ts, (nl - 1) * h + l - 1) if l > 1 else None
                        T = blocks(k.T[:, :, :], l, 0)
                        dve.tensor_tensor(T, T, blocks(bank[5], l, 0), ALU.subtract).then_inc(s.Ts, 1)
                    if follow and l == 2:
                        conv(h + 1, 0, 1 - par)
                    if l == 3:
                        dve.wait_ge(s.v_turned, h + 1)
                        dve.tensor_tensor(k.vb[:, :, :], four(bank[7][:, :]), bcast(head_of(k.beta, h), 2, P),
                                          ALU.mult).then_inc(s.tok, 1)
                    if follow and l == 4:
                        decays(h + 1)
                    if follow and l == 5:
                        conv(h + 1, 1, 1 - par)
                for t in range(NT - 1):
                    dve.wait_ge(s.dS, 3 * h + t + 1)
                    new, old = k.state[:, t % 2, :], k.state[:, (t - 1) % 2, :]
                    if t == 0:
                        dve.tensor_copy(new, tile(bank[4], 0)).then_inc(s.St, 1)
                    else:
                        dve.wait_ge(s.St, 3 * h + t)
                        dve.scalar_tensor_tensor(new, old, head_of(k.eGlast, h)[:, t:t + 1], tile(bank[4], t),
                                                 ALU.mult, ALU.add).then_inc(s.St, 1)
                    if follow and t == NT - 2:
                        conv(h + 1, 2, 1 - par)
                if follow:
                    normalise(h + 1, 0, 1 - par)
                    normalise(h + 1, 1, 1 - par)
                dve.wait_ge(s.rn, 3 * h + 3 + (2 if follow else 0))
                link(dve.scalar_tensor_tensor(k.og[:, :], bank[7][:, :], k.g_o[:, 0:1], k.rnorm[:, 2, :], ALU.mult,
                                              ALU.mult))
                dve.wait_ge(s.sil, 4 * h + 4)
                dve.tensor_tensor(k.oT[:, bass.ds(h, 1), :].rearrange("p h n -> p (h n)"), k.og[:, :],
                                  k.qkvz[:, par, 3, :], ALU.mult).then_inc(s.og, 1)
                assert n == VSTEPS

            VSTEPS = 5
            for j in range(3):
                conv(0, j, 0)
            decays(0)
            normalise(0, 0, 0)
            normalise(0, 1, 0)
            head(0, 0)
            head(1, 1)
            with dve.Fori(1, HEADS // 2 - 1) as i:
                head(2 * i, 0)
                head(2 * i + 1, 1)
            head(HEADS - 2, 0)
            head(HEADS - 1, 1, follow=False)

        @block.scalar
        def _(act):
            def silu(h, j, par):
                if j < 3:
                    act.wait_ge(s.conv, 3 * h + j + 1)
                    src = k.cv[:, j, :]
                else:
                    act.wait_ge(s.proj, 4 * h + 4)
                    src = bank[1][:, :]
                act.activation(k.qkvz[:, par, j, :], src, ACT.Silu).then_inc(s.sil, 1)
                if j < 2:
                    act.wait_ge(s.sil, 4 * h + j + 1)
                    act.activation(k.sqr[:, j, :], k.qkvz[:, par, j, :], ACT.Square).then_inc(s.sq, 1)

            def logs(h, which, count):
                for j in which:
                    if j == 2:
                        act.wait_ge(s.oss, h + 1)
                        act.activation(k.rnorm[:, 2, :], bank[4][:, :], ACT.Ln, bias=k.eps[:, 0:1],
                                       scale=1.0 / DK).then_inc(s.ln, 1)
                    else:
                        act.wait_ge(s.ssq, 2 * (h + 1) + j + 1 if count else j + 1)
                        act.activation(k.rnorm[:, j, :], bank[(2, 5)[j]][:, :], ACT.Ln,
                                       bias=k.eps[:, 0:1]).then_inc(s.ln, 1)

            def exps(h, which, done):
                act.wait_ge(s.ln, done)
                for j in which:
                    act.activation(k.rnorm[:, j, :], k.rnorm[:, j, :], ACT.Exp, scale=-0.5).then_inc(s.rn, 1)

            def head(h, par, follow=True):
                act.wait_ge(s.clip, 2 * h + 1)
                act.activation(k.lo[:, :, :], k.lo[:, :, :], ACT.Exp, scale=-1.0).then_inc(s.dec, 1)
                act.wait_ge(s.clip, 2 * h + 2)
                act.activation(k.hi[:, :, :], k.hi[:, :, :], ACT.Exp).then_inc(s.dec, 1)
                act.activation(k.eGrow[:, :], bank[5][:, :], ACT.Exp).then_inc(s.eg, 1)
                act.wait_ge(s.Vt, h + 1)
                act.activation(k.V[:, :, :], four(bank[3][:, :]), ACT.Copy).then_inc(s.V0, 1)
                for l in range(1, LEVELS):
                    act.wait_ge(s.X, nl * h + l)
                    act.activation(k.X[:, :, :], four(bank[3][:, :]), ACT.Copy).then_inc(s.Xs, 1)
                    if l == 1:
                        silu(h, 2, par)
                        silu(h, 3, par)
                    if follow and l == 3:
                        silu(h + 1, 0, 1 - par)
                    if follow and l == LEVELS - 1:
                        silu(h + 1, 1, 1 - par)
                act.wait_ge(s.W, h + 1)
                act.activation(k.nWT[:, :], bank[6][:, :], ACT.Copy, scale=-1.0).then_inc(s.nW, 1)
                for t in range(NT):
                    act.wait_ge(s.u, 4 * h + t + 1)
                    act.activation(k.us[:, t, :], tile(bank[3], t), ACT.Copy).then_inc(s.us, 1)
                act.wait_ge(s.o, h + 1)
                act.activation(k.osq[:, :], bank[7][:, :], ACT.Square).then_inc(s.osq, 1)
                if follow:
                    logs(h, (0, 1, 2), True)
                    exps(h, (0, 1, 2), 3 * h + 5)
                else:
                    logs(h, (2,), True)
                    exps(h, (2,), 3 * h + 3)

            silu(0, 0, 0)
            silu(0, 1, 0)
            logs(0, (0, 1), False)
            exps(0, (0, 1), 2)
            head(0, 0)
            head(1, 1)
            with act.Fori(1, HEADS // 2 - 1) as i:
                head(2 * i, 0)
                head(2 * i + 1, 1)
            head(HEADS - 2, 0)
            head(HEADS - 1, 1, follow=False)

        @block.gpsimd
        def _(pool):
            def head(h):
                pool.wait_ge(s.L, h + 1)
                for l in range(1, LEVELS):
                    pool.tensor_tensor(k.C[:, l, :, :], k.lo[:, :, :], bcast(k.join[:, l, :], 1, NT),
                                       ALU.mult).then_inc(s.C, 1)

            head(0)
            with pool.Fori(1, HEADS) as h:
                head(h)

        @block.sync
        def _(sp):
            def load(h, slot):
                sp.wait_ge(s.proj, 4 * (h - 1))
                dst, src = load_head(k, h, slot)
                sp.dma_start(dst, src).then_inc(R.landed[slot], 16)

            with sp.Fori(1, HEADS // 2) as i:
                load(2 * i, 0)
                load(2 * i + 1, 1)
            following(sp)


def project_out(k, tag, xT, chunks, slots_of, following):
    done, added = k.sem(f"{tag}_done"), k.sem(f"{tag}_added")
    with nc_block(k) as block:

        @block.tensor
        def _(pe):
            for n in range(2):
                w = slots_of(pe, n)
                for t in range(NT):
                    for c in range(chunks):
                        last = pe.matmul(k.bank[n * NT + t][:, :], xT[:, c, t * P:(t + 1) * P], w(c), start=(c == 0),
                                         stop=(c == chunks - 1))
                    last.then_inc(done, 1)

        @block.vector
        def _(dve):
            for j in range(2 * NT):
                dve.wait_ge(done, j + 1)
                out = k.H[:, j % NT, j // NT * HALF:(j // NT + 1) * HALF]
                dve.tensor_tensor(out, out, k.bank[j][:, :], ALU.add).then_inc(added, 1)

        @block.sync
        def _(sp):
            following(sp, done)



NSCORE = SEQ + 2 * P


def head_features(k, tag, gain, w_of, ntiles, out, norm_gain, first_slots, following, values=None, scale=None,
                  fresh=True):
    s = norm_semaphores(k, tag)
    (s.proj, s.sq, s.sums, s.ln, s.rn, s.out, s.scaled, s.vproj, s.v) = (
        k.sem(f"{tag}_{name}") for name in
        ("proj", "sq", "sums", "ln", "rn", "out", "scaled", "vproj", "v"))
    bank = k.bank
    with nc_block(k) as block:

        @block.tensor
        def _(pe):
            norm_tensor(pe, k, s, fresh)

            def sums(j):
                pe.wait_ge(s.sq, j + 1)
                if j >= 2:
                    pe.wait_ge(s.ln, j - 1)
                pe.matmul(bank[4 + j % 2][:, :], k.ones, k.sqr[:, j % 2, :], start=True, stop=True).then_inc(s.sums, 1)

            for j in range(ntiles):
                w = w_of(pe, j)
                if j >= 4:
                    pe.wait_ge(s.out, j - 3)
                for c in range(DC):
                    if j == 0:
                        norm_chunk(pe, s, c)
                    last = pe.matmul(bank[j % 4][:, :], w[:, c, :], k.xnT[:, c, :], start=(c == 0),
                                     stop=(c == DC - 1))
                last.then_inc(s.proj, 1)
                if j:
                    sums(j - 1)
            sums(ntiles - 1)
            if values:
                values.tensor(pe, s)
            for n, slot in enumerate(first_slots):
                k.R.takes[slot] += 1
                if values:
                    k.R.free[slot] = (s.vproj, (n + 1) * NT)
                else:
                    k.R.free[slot] = (s.proj, (n + 1) * QPG)

        @block.scalar
        def _(act):
            norm_scalar(act, k, s, gain, fresh)

            def root(j):
                act.wait_ge(s.sums, j + 1)
                if j >= 2:
                    act.wait_ge(s.out, j - 1)
                act.activation(k.rnorm[:, j % 2, :], bank[4 + j % 2][:, :], ACT.Ln, bias=k.eps,
                               scale=1.0 / HD).then_inc(s.ln, 1)
                act.wait_ge(s.ln, j + 1)
                act.activation(k.rnorm[:, j % 2, :], k.rnorm[:, j % 2, :], ACT.Exp, scale=-0.5).then_inc(s.rn, 1)

            for j in range(ntiles):
                act.wait_ge(s.proj, j + 1)
                if j >= 2:
                    act.wait_ge(s.sums, j - 1)
                act.activation(k.sqr[:, j % 2, :], bank[j % 4][:, :], ACT.Square).then_inc(s.sq, 1)
                if j:
                    root(j - 1)
            root(ntiles - 1)

        @block.vector
        def _(dve):
            norm_vector(dve, k, s, gain, fresh)
            if scale:
                dve.tensor_scalar(norm_gain, norm_gain, scale, None, ALU.mult).then_inc(s.scaled, 1)
                dve.wait_ge(s.scaled, 1)
            for j in range(ntiles):
                g = j * GROUPS // ntiles
                dve.wait_ge(s.rn, j + 1)
                dve.scalar_tensor_tensor(out[:, j, :], bank[j % 4][:, :], norm_gain[:, g:g + 1],
                                         k.rnorm[:, j % 2, :], ALU.mult, ALU.mult).then_inc(s.out, 1)
            if values:
                values.vector(dve, s)

        @block.sync
        def _(sp):
            following(sp)


class Values:

    def __init__(self, k):
        self.k = k

    def tensor(self, pe, s):
        k = self.k
        for g in range(GROUPS):
            w = k.R.flat(3 + g).rearrange("p (c n) -> p c n", c=DC)[:, :, KVPG * HD:]
            for d in range(NT):
                n = g * NT + d
                if n >= 2:
                    pe.wait_ge(s.v, n - 1)
                for c in range(DC):
                    x = k.xnT[:, c, d * P:(d + 1) * P] if g == 0 else k.xnT[:, c, d::4]
                    last = pe.matmul(k.bank[6 + n % 2][:, 0:KVPG * HD], x, w[:, c, :], start=(c == 0),
                                     stop=(c == DC - 1))
                last.then_inc(s.vproj, 1)

    def vector(self, dve, s):
        k = self.k
        for n in range(GROUPS * NT):
            dve.wait_ge(s.vproj, n + 1)
            dve.tensor_copy(k.V[:, n // NT, n % NT, :], k.bank[6 + n % 2][:, 0:KVPG * HD]).then_inc(s.v, 1)


def attend(k, following):
    s = Net()
    (s.dist, s.S, s.biased, s.peak, s.exp, s.inv, s.prob, s.turned, s.PTa, s.PTb, s.O, s.out) = (
        k.sem(f"at_{name}") for name in
        ("dist", "S", "biased", "peak", "exp", "inv", "prob", "turned", "PTa", "PTb", "O", "out"))
    bank = k.bank
    blocks = [(qh, d) for qh in range(QPG) for d in range(4)]
    NB = len(blocks)
    slope = lambda g, qh: 2.0 ** (-8.0 * (g * QPG + qh + 1) / (GROUPS * QPG))
    with nc_block(k) as block:

        @block.tensor
        def _(pe):
            def scores(b):
                qh, d = blocks[b]
                kv = qh // 2
                if b >= 2:
                    pe.wait_ge(s.biased, 2 * (b - 1))
                pe.matmul(bank[b % 2][:, :], k.qT[:, qh, d::4], k.kT[:, kv, :], start=True, stop=True)
                for g in (1, 2):
                    last = pe.matmul(bank[2 + b % 2][:, (g - 1) * P:g * P], k.qT[:, g * QPG + qh, d::4],
                                     k.kT[:, g * KVPG + kv, d::4], start=True, stop=True)
                last.then_inc(s.S, 1)

            scores(0)
            scores(1)
            for b in range(NB):
                qh, d = blocks[b]
                kv = qh // 2
                pe.wait_ge(s.prob, b + 1)
                wait(pe, s.PTa, b)
                wait(pe, s.PTb, b)
                for n in range(6):
                    last = pe.transpose(bank[4 + n // 4][:, n % 4 * P:(n % 4 + 1) * P],
                                        k.sc[:, b % 2, n * P:(n + 1) * P], k.ident)
                last.then_inc(s.turned, 1)
                if b + 2 < NB:
                    scores(b + 2)
                pe.wait_ge(s.PTa, b + 1)
                pe.wait_ge(s.PTb, b + 1)
                if b >= 2:
                    pe.wait_ge(s.out, b - 1)
                for n in range(6):
                    v = k.V[:, 0, n] if n < 4 else k.V[:, n - 3, d]
                    last = pe.matmul(bank[6 + b % 2][:, 0:P], v[:, kv * HD:(kv + 1) * HD],
                                     k.PT[:, n * P:(n + 1) * P], start=(n == 0), stop=(n == 5))
                last.then_inc(s.O, 1)

        @block.vector
        def _(dve):
            dve.wait_ge(s.dist, 16)

            def softmax(b):
                qh, d = blocks[b]
                sc = k.sc[:, b % 2, :]
                dve.wait_ge(s.S, b + 1)
                if b >= 2:
                    dve.wait_ge(s.turned, b - 1)
                dve.scalar_tensor_tensor(sc[:, 0:SEQ], k.dist[:, d * SEQ:(d + 1) * SEQ], -slope(0, qh), bank[b % 2][:, :],
                                         ALU.mult, ALU.add)
                for g in (1, 2):
                    last = dve.scalar_tensor_tensor(sc[:, SEQ + (g - 1) * P:SEQ + g * P],
                                                    k.dist[:, 4 * SEQ + (g - 1) * P:4 * SEQ + g * P], -slope(g, qh),
                                                    bank[2 + b % 2][:, (g - 1) * P:g * P], ALU.mult, ALU.add)
                    if g == 1:
                        last.then_inc(s.biased, 1)
                last.then_inc(s.biased, 1)
                dve.wait_ge(s.biased, 2 * b + 2)
                dve.tensor_reduce(k.peak[:, b % 2:b % 2 + 1], sc, AX.X, ALU.max, negate=True).then_inc(s.peak, 1)

            def normalise(b):
                dve.wait_ge(s.exp, b + 1)
                dve.reciprocal(k.inv[:, b % 2:b % 2 + 1], k.total[:, b % 2:b % 2 + 1]).then_inc(s.inv, 1)
                dve.wait_ge(s.inv, b + 1)
                dve.tensor_scalar(k.sc[:, b % 2, :], k.sc[:, b % 2, :], k.inv[:, b % 2:b % 2 + 1], None,
                                  ALU.mult).then_inc(s.prob, 1)

            softmax(0)
            softmax(1)
            normalise(0)
            for b in range(NB):
                dve.wait_ge(s.turned, b + 1)
                if b:
                    dve.wait_ge(s.O, b)
                dve.tensor_copy(k.PT[:, SEQ:], bank[5][:, 0:2 * P]).then_inc(s.PTb, 1)
                if b + 1 < NB:
                    normalise(b + 1)
                if b + 2 < NB:
                    softmax(b + 2)

        @block.scalar
        def _(act):
            def exps(b):
                act.wait_ge(s.peak, b + 1)
                sc = k.sc[:, b % 2, :]
                act.activation(sc, sc, ACT.Exp, bias=k.peak[:, b % 2:b % 2 + 1],
                               accum_out=k.total[:, b % 2:b % 2 + 1]).then_inc(s.exp, 1)

            exps(0)
            exps(1)
            for b in range(NB):
                qh, d = blocks[b]
                act.wait_ge(s.turned, b + 1)
                if b:
                    act.wait_ge(s.O, b)
                act.activation(k.PT[:, 0:SEQ], bank[4][:, :], ACT.Copy).then_inc(s.PTa, 1)
                if b + 2 < NB:
                    exps(b + 2)
                act.wait_ge(s.O, b + 1)
                act.activation(k.aoT[:, qh, d::4], bank[6 + b % 2][:, 0:P], ACT.Copy).then_inc(s.out, 1)

        @block.sync
        def _(sp):
            sp.dma_start(k.dist[:, :], k.dist_d).then_inc(s.dist, 16)
            following(sp)




def route(k, layer, following):
    tag = f"rt{layer}"
    s = norm_semaphores(k, tag)
    gain = k.g_ffn[:, layer, :]
    (s.hi, s.res1, s.mid, s.res2, s.lo, s.logits, s.gdiff, s.gexp, s.ediff, s.eexp, s.chosen, s.ranks, s.steps) = (
        k.sem(f"{tag}_{name}") for name in
        ("hi", "res1", "mid", "res2", "lo", "logits", "gdiff", "gexp", "ediff", "eexp", "chosen", "ranks",
         "steps"))
    lg, el, eq = k.lg, k.el, k.eq
    with nc_block(k) as block:

        @block.tensor
        def _(pe):
            norm_tensor(pe, k, s)
            norm_chunk(pe, s, 2)
            norm_chunk(pe, s, 3)
            for c in range(DC):
                norm_chunk(pe, s, c)
                for t in range(NT):
                    last = pe.matmul(k.bank[t][:, 0:MG + EXPERTS], k.xnT[:, c, t * P:(t + 1) * P],
                                     k.w_router[:, layer, c, :], start=(c == 0), stop=(c == DC - 1))
            last.then_inc(s.logits, 1)
            pe.wait_ge(s.chosen, 1)
            for t in range(NT):
                out = k.bank[1][:, t * EXPERTS:(t + 1) * EXPERTS]
                for u in range(t):
                    pe.matmul(out, k.ones_b, k.M[:, u, :], start=(u == 0), stop=False)
                pe.matmul(out, k.before_b, k.M[:, t, :], start=(t == 0), stop=True)
            out = k.bank[1][:, NT * EXPERTS:(NT + 1) * EXPERTS]
            for u in range(NT):
                last = pe.matmul(out, k.ones_b, k.M[:, u, :], start=(u == 0), stop=(u == NT - 1))
            last.then_inc(s.ranks, 1)

        @block.scalar
        def _(act):
            def highest():
                for t in range(NT):
                    act.wait_ge(s.xn_odd if t % 2 else s.xn, t // 2 + 1)
                    act.activation(k.xs[:, 0, t, :], k.xn[:, t, :], ACT.Copy).then_inc(s.hi, 1)

            def lowest(t):
                act.wait_ge(s.res2, t + 1)
                act.activation(k.xs[:, 2, t, :], k.xn[:, t, :], ACT.Copy).then_inc(s.lo, 1)

            norm_scalar(act, k, s, gain, meanwhile=highest)
            for t in range(NT):
                act.wait_ge(s.res1, t + 1)
                act.activation(k.xs[:, 1, t, :], k.xn[:, t, :], ACT.Copy).then_inc(s.mid, 1)
            act.wait_ge(s.gdiff, 1)
            act.activation(k.ge[:, :, :], k.gd[:, :, :], ACT.Exp).then_inc(s.gexp, 1)
            lowest(0)
            lowest(1)
            act.wait_ge(s.ediff, 1)
            act.activation(k.e2[:, :], k.ed[:, :], ACT.Exp).then_inc(s.eexp, 1)
            lowest(2)
            lowest(3)

        @block.gpsimd
        def _(pool):
            pool.wait_ge(s.turned, DC)
            for t in range(NT):
                pool.wait_ge(s.hi, t + 1)
                pool.tensor_tensor(k.xn[:, t, :], k.xn[:, t, :], k.xs[:, 0, t, :], ALU.subtract).then_inc(s.res1, 1)
            for t in range(NT):
                pool.wait_ge(s.mid, t + 1)
                pool.tensor_tensor(k.xn[:, t, :], k.xn[:, t, :], k.xs[:, 1, t, :], ALU.subtract).then_inc(s.res2, 1)

        @block.vector
        def _(dve):
            norm_vector(dve, k, s, gain)
            ch = Chain(dve, s.steps)
            dve.wait_ge(s.logits, 1)
            for t in range(NT):
                logits = dve.tensor_tensor(lg[:, t, :], k.bank[t][:, 0:MG + EXPERTS], k.b_router[:, layer, :], ALU.add)
            ch.link(logits)
            gl = lg[:, :, 0:MG]
            ch.link(dve.tensor_reduce(k.gm[:, :], gl, AX.X, ALU.max))
            dve.tensor_tensor(k.gd[:, :, :], gl, bcast(k.gm[:, :], 2, MG), ALU.subtract).then_inc(s.gdiff, 1)
            ch.link(dve.tensor_tensor(k.gq[:, :, :], gl, bcast(k.gm[:, :], 2, MG), ALU.is_equal))
            ch.link(dve.tensor_tensor(k.gq[:, :, :], k.gq[:, :, :], bcast(k.first[:, 0:MG], 1, NT), ALU.mult))
            ch.link(dve.tensor_reduce(k.gs[:, :], k.gq[:, :, :], AX.X, ALU.max))
            ch.link(dve.tensor_tensor(k.gq[:, :, :], k.gq[:, :, :], bcast(k.gs[:, :], 2, MG), ALU.is_equal))
            ch.link(dve.tensor_scalar(k.gq[:, :, :], k.gq[:, :, :], 1.0, BIG, ALU.subtract, ALU.mult))
            ch.link(dve.tensor_tensor(
                el[:, :, :].rearrange("p t (g e) -> p t g e", g=MG),
                lg[:, :, MG:].rearrange("p t (g e) -> p t g e", g=MG),
                bcast(k.gq[:, :, :], 3, ME), ALU.add))

            def best(m, onehot):
                ch.link(dve.tensor_reduce(m, el[:, :, :], AX.X, ALU.max))
                ch.link(dve.tensor_tensor(eq[:, :, :], el[:, :, :], bcast(m, 2, EXPERTS), ALU.is_equal))
                ch.link(dve.tensor_tensor(eq[:, :, :], eq[:, :, :], bcast(k.first[:, 0:EXPERTS], 1, NT), ALU.mult))
                ch.link(dve.tensor_reduce(k.gs[:, :], eq[:, :, :], AX.X, ALU.max))
                ch.link(dve.tensor_tensor(onehot, eq[:, :, :], bcast(k.gs[:, :], 2, EXPERTS), ALU.is_equal))

            best(k.m1[:, :], k.oh1[:, :, :])
            ch.link(dve.scalar_tensor_tensor(el[:, :, :], k.oh1[:, :, :], -BIG, el[:, :, :], ALU.mult, ALU.add))
            best(k.m2[:, :], k.oh2[:, :, :])
            dve.tensor_tensor(k.ed[:, :], k.m2[:, :], k.m1[:, :], ALU.subtract).then_inc(s.ediff, 1)
            dve.tensor_tensor(k.M[:, :, :], k.oh1[:, :, :], k.oh2[:, :, :], ALU.add).then_inc(s.chosen, 1)
            dve.wait_ge(s.gexp, 1)
            ch.link(dve.tensor_reduce(k.gs[:, :], k.ge[:, :, :], AX.X, ALU.add))
            dve.wait_ge(s.eexp, 1)
            ch.link(dve.scalar_tensor_tensor(k.gs[:, :], k.e2[:, :], 1.0, k.gs[:, :], ALU.add, ALU.mult))
            ch.link(dve.reciprocal(k.c1[:, :], k.gs[:, :]))
            ch.link(dve.tensor_tensor(k.c2[:, :], k.c1[:, :], k.e2[:, :], ALU.mult))
            ch.link(dve.tensor_tensor(k.oh1[:, :, :], k.oh1[:, :, :], bcast(k.c1[:, :], 2, EXPERTS), ALU.mult))
            ch.link(dve.tensor_tensor(k.oh2[:, :, :], k.oh2[:, :, :], bcast(k.c2[:, :], 2, EXPERTS), ALU.mult))
            ch.link(dve.tensor_tensor(k.Wt[:, :, :], k.oh1[:, :, :], k.oh2[:, :, :], ALU.add))
            dve.wait_ge(s.chosen, 1)
            ch.link(dve.tensor_scalar(k.rank[:, :, :], k.M[:, :, :], NOT_CHOSEN, NOT_CHOSEN, ALU.mult, ALU.subtract))
            dve.wait_ge(s.ranks, 1)
            raw = k.bank[1][:, 0:NT * EXPERTS].rearrange("p (t e) -> p t e", t=NT)
            ch.link(dve.tensor_tensor(k.rank[:, :, :], k.rank[:, :, :], raw, ALU.add))
            total = k.bank[1][:, NT * EXPERTS:(NT + 1) * EXPERTS]
            ch.link(dve.tensor_reduce(k.most[:, :], total, AX.X, ALU.max))
            ch.link(dve.tensor_scalar(k.most_i[:, :], k.most[:, :], 1.0, None, ALU.subtract))
            dve.tensor_scalar(k.extra[:, layer:layer + 1], k.most_i[:, :], SLOTS.bit_length() - 1,
                              None, ALU.logical_shift_right).then_inc(s.steps, 1)

        @block.sync
        def _(sp):
            following(sp)


def expert_semaphores(k, tag):
    s = Net()
    (s.half0, s.half2, s.half4, s.slots, s.weighted, s.shift, s.gathered, s.xT, s.h1, s.h3, s.silu, s.hidden,
     s.hidden_turned, s.hT, s.S_turned, s.S, s.yps, s.y, s.spread, s.added) = (
         k.sem(f"{tag}_{name}") for name in
         ("half0", "half2", "half4", "slots", "weighted", "shift", "gathered", "xT", "h1", "h3", "silu",
          "hidden", "hidden_turned", "hT", "S_turned", "S", "yps", "y", "spread", "added"))
    return s


def build_slots(dve, k, s, pair, i, reuse):
    if reuse:
        wait(dve, s.gathered, 2 * i)
        wait(dve, s.weighted, i)
    ranks = k.rank[:, :, bass.ds(pair * 2, 2)]
    if not (isinstance(i, int) and i == 0):
        wait(dve, s.shift, i)
    dve.tensor_tensor(
        k.slot1h[:, :, :].rearrange("p t (e n) -> p t e n", e=2), bcast(ranks, 3, SLOTS),
        bcast(bcast(k.iota[:, 0:SLOTS], 1, 2), 1, NT), ALU.is_equal).then_inc(s.slots, 1)
    wait(dve, s.slots, i + 1)
    dve.tensor_scalar(ranks, ranks, float(SLOTS), None, ALU.subtract).then_inc(s.shift, 1)


def weigh_slots(dve, k, s, pair, i):
    wait(dve, s.S_turned, i)
    wait(dve, s.slots, i + 1)
    dve.tensor_tensor(
        k.slotw[:, :, :].rearrange("p t (e n) -> p t e n", e=2),
        k.slot1h[:, :, :].rearrange("p t (e n) -> p t e n", e=2),
        bcast(k.Wt[:, :, bass.ds(pair * 2, 2)], 3, SLOTS), ALU.mult).then_inc(s.weighted, 1)


def evacuate_gather(dve, k, s, layer, i):
    for half in range(2):
        wait(dve, s.gathered, 2 * i + half + 1)
        gain = k.g_ffn[:, layer, 4 * half:4 * half + 4]
        dve.tensor_tensor(k.xT[:, 4 * half:4 * half + 4, :],
                          k.bank[6 + half][:, :].rearrange("p (c n) -> p c n", c=4),
                          bcast(gain, 2, P), ALU.mult).then_inc(s.xT, 1)


def hidden(dve, k, s, i):
    dve.wait_ge(s.silu, i + 1)
    dve.wait_ge(s.h3, i + 1)
    dve.tensor_tensor(k.h[:, :], k.h1s[:, :], k.bank[1][:, :], ALU.mult).then_inc(s.hidden, 1)


def add_results(dve, k, s, i):
    for n in range(2):
        for t in range(NT):
            j = n * NT + t
            dve.wait_ge(s.spread, 8 * i + j + 1)
            out = k.H[:, t, n * HALF:(n + 1) * HALF]
            dve.tensor_tensor(out, out, k.bank[6 + j % 2][:, :], ALU.add).then_inc(s.added, 1)


def gather(pe, k, s, i, after):
    pe.wait_ge(s.slots, i + 1)
    wait(pe, s.added, after)
    for half in range(2):
        for c in range(4 * half, 4 * half + 4):
            n = 0
            for part in range(3):
                for t in range(NT):
                    last = pe.matmul(k.bank[6 + half][:, (c % 4) * P:(c % 4 + 1) * P], k.xs[:, part, t, c::DC],
                                     k.slot1h[:, t, :], start=(n == 0), stop=(n == 3 * NT - 1))
                    n += 1
        last.then_inc(s.gathered, 1)


def expert_matmuls(pe, k, arrived, m, x, chunks, out, cols, half, done):
    per = chunks // 2
    for c in range(chunks):
        slot = 2 * m + c // per
        if arrived and c % per == 0:
            arrived(slot)
        w = k.ring[:, slot, :].rearrange("p (e c n) -> p e c n", e=2, c=per)
        for e in range(2):
            last = pe.matmul(out[e * SLOTS:(e + 1) * SLOTS, :], x[:, c, e * SLOTS:(e + 1) * SLOTS],
                             w[:, e, c % per, cols], start=(c == 0), stop=(c == chunks - 1))
        if half and c == per - 1:
            last.then_inc(half, 1)
    last.then_inc(done, 1)


def expert_up(pe, k, s, i, arrived):
    pe.wait_ge(s.xT, 2 * i + 2)
    wait(pe, s.S, i)
    expert_matmuls(pe, k, arrived, 0, k.xT, DC, k.bank[0], slice(0, FF), s.half0, s.h1)
    expert_matmuls(pe, k, arrived, 1, k.xT, DC, k.bank[1], slice(0, FF), s.half2, s.h3)


def expert_turn(pe, k, s, i):
    pe.wait_ge(s.hidden, i + 1)
    for c in range(FC):
        last = pe.transpose(k.bank[4][:, c * P:(c + 1) * P], k.h[:, c::FC], k.ident)
    last.then_inc(s.hidden_turned, 1)
    pe.wait_ge(s.weighted, i + 1)
    for t in range(NT):
        last = pe.transpose(k.bank[0][:, t * P:(t + 1) * P], k.slotw[:, t, :], k.ident)
    last.then_inc(s.S_turned, 1)


def expert_down(pe, k, s, i, arrived):
    pe.wait_ge(s.hT, i + 1)
    for n in range(2):
        expert_matmuls(pe, k, None if n else arrived, 2, k.hT, FC, k.bank[2 + n],
                       slice(n * HALF, (n + 1) * HALF), s.half4 if n else None, s.yps)


def spread(pe, k, s, i, evacuated):
    pe.wait_ge(s.S, i + 1)
    pe.wait_ge(s.xT, evacuated)
    for n in range(2):
        pe.wait_ge(s.y, 2 * i + n + 1)
        for t in range(NT):
            j = n * NT + t
            if j >= 2:
                pe.wait_ge(s.added, 8 * i + j - 1)
            pe.matmul(k.bank[6 + j % 2][:, :], k.S[:, t * P:(t + 1) * P], k.y[:, n * HALF:(n + 1) * HALF],
                      start=True, stop=True).then_inc(s.spread, 1)


def expert_scalar(act, k, s, i):
    act.wait_ge(s.h1, i + 1)
    wait(act, s.hidden, i)
    act.activation(k.h1s[:, :], k.bank[0][:, :], ACT.Silu).then_inc(s.silu, 1)
    act.wait_ge(s.hidden_turned, i + 1)
    act.activation(k.hT[:, :, :], k.bank[4][:, :].rearrange("p (c n) -> p c n", c=FC), ACT.Copy).then_inc(s.hT, 1)
    act.wait_ge(s.S_turned, i + 1)
    act.activation(k.S[:, :], k.bank[0][:, :], ACT.Copy).then_inc(s.S, 1)
    for n in range(2):
        act.wait_ge(s.yps, 2 * i + n + 1)
        act.activation(k.y[:, n * HALF:(n + 1) * HALF], k.bank[2 + n][:, :], ACT.Copy).then_inc(s.y, 1)


def experts(k, layer, following):
    s = expert_semaphores(k, f"mx{layer}")
    R = k.R
    frees = ((s.half0, 1), (s.h1, 1), (s.half2, 1), (s.h3, 1), (s.half4, 1), (s.yps, 2))
    with nc_block(k) as block:

        @block.tensor
        def _(pe):
            def pair(i, last=False):
                def arrived(slot):
                    R.arrived(pe, slot, i)

                expert_up(pe, k, s, i, arrived)
                if not last:
                    gather(pe, k, s, i + 1, 8 * i)
                expert_turn(pe, k, s, i)
                expert_down(pe, k, s, i, arrived)
                spread(pe, k, s, i, 2 * i + (2 if last else 4))

            gather(pe, k, s, 0, 0)
            pair(0)
            with pe.Fori(1, PAIRS - 1) as i:
                pair(i)
            pair(PAIRS - 1, last=True)
            for slot in range(RING):
                R.takes[slot] += PAIRS
                R.free[slot] = (frees[slot][0], PAIRS * frees[slot][1])

        @block.vector
        def _(dve):
            def pair(i, last=False):
                weigh_slots(dve, k, s, i, i)
                if not last:
                    build_slots(dve, k, s, i + 1, i + 1, True)
                hidden(dve, k, s, i)
                if not last:
                    evacuate_gather(dve, k, s, layer, i + 1)
                add_results(dve, k, s, i)

            build_slots(dve, k, s, 0, 0, False)
            evacuate_gather(dve, k, s, layer, 0)
            pair(0)
            with dve.Fori(1, PAIRS - 1) as i:
                pair(i)
            pair(PAIRS - 1, last=True)

        @block.scalar
        def _(act):
            expert_scalar(act, k, s, 0)
            with act.Fori(1, PAIRS) as i:
                expert_scalar(act, k, s, i)

        @block.sync
        def _(sp):
            with sp.Fori(1, PAIRS) as i:
                def load(slot, dst, src):
                    sem, per = frees[slot]
                    sp.wait_ge(sem, i * per)
                    sp.dma_start(dst, src).then_inc(R.landed[slot], 16)

                load_expert_pair(k, layer, i, load)
            extra = sp.value_load(k.extra[0:1, layer:layer + 1], min_val=0, max_val=SEQ // SLOTS - 1)
            with sp.If(extra < 1):
                following(sp)


def more_experts(k, layer, following):
    s = expert_semaphores(k, f"my{layer}")
    landed, done = k.sem(f"my{layer}_landed"), k.sem(f"my{layer}_done")

    def loop(eng, body):
        extra = eng.value_load(k.extra[0:1, layer:layer + 1], min_val=0, max_val=SEQ // SLOTS - 1)
        with eng.If(extra > 0):
            with eng.Fori(0, extra) as p:
                with eng.Fori(0, PAIRS) as pair:
                    i = p * PAIRS + pair
                    eng.wait_ge(done, i + 1)
                    body(i, pair)

    with nc_block(k) as block:

        @block.tensor
        def _(pe):
            def step(i, pair):
                def arrived(slot):
                    pe.wait_ge(landed, (i + 1) * (16 * RING))

                gather(pe, k, s, i, 0)
                expert_up(pe, k, s, i, arrived)
                expert_turn(pe, k, s, i)
                expert_down(pe, k, s, i, arrived)
                spread(pe, k, s, i, 2 * i + 2)

            loop(pe, step)

        @block.vector
        def _(dve):
            dve.sem_inc(done, 1)

            def step(i, pair):
                build_slots(dve, k, s, pair, i, True)
                weigh_slots(dve, k, s, pair, i)
                evacuate_gather(dve, k, s, layer, i)
                hidden(dve, k, s, i)
                add_results(dve, k, s, i)
                dve.wait_ge(s.added, 8 * i + 8)
                dve.sem_inc(done, 1)

            loop(dve, step)

        @block.scalar
        def _(act):
            loop(act, lambda i, pair: expert_scalar(act, k, s, i))

        @block.sync
        def _(sp):
            def load(slot, dst, src):
                sp.dma_start(dst, src).then_inc(landed, 16)

            loop(sp, lambda i, pair: load_expert_pair(k, layer, pair, load))
            extra = sp.value_load(k.extra[0:1, layer:layer + 1], min_val=0, max_val=SEQ // SLOTS - 1)
            with sp.If(extra > 0):
                sp.wait_ge(done, extra * PAIRS + 1)
                following(sp)




def embed(k, layer, following, store=False):
    tag = f"pe{layer}"
    s = norm_semaphores(k, tag)
    (s.gate, s.sig, s.prod, s.sum, s.p) = (
        k.sem(f"{tag}_{name}") for name in
        ("gate", "sig", "prod", "sum", "p"))
    R = k.R
    gain = k.g_ple[:, layer, :]
    with nc_block(k) as block:

        @block.tensor
        def _(pe):
            norm_tensor(pe, k, s)
            pe.wait_ge(s.p, 16)
            norm_chunk(pe, s, DC - 2)
            norm_chunk(pe, s, DC - 1)
            wp = R.flat(2, 2048).rearrange("p (c n) -> p c n", c=2)
            for n in range(2):
                R.arrived(pe, n)
                w = R.flat(n).rearrange("p (c n) -> p c n", c=DC)
                for t in range(NT):
                    j = n * NT + t
                    if j >= 4:
                        pe.wait_ge(s.prod, j - 3)
                    for c in range(DC):
                        pe.matmul(k.bank[j % 4][:, :], k.xnT[:, c, t * P:(t + 1) * P], w[:, c, :],
                                  start=(c == 0), stop=(c == DC - 1))
                    if j == 0:
                        R.arrived(pe, 2)
                    for c in range(2):
                        g = pe.matmul(k.bank[4 + j % 4][:, :], k.pT[:, c, t * P:(t + 1) * P],
                                      wp[:, c, n * HALF:(n + 1) * HALF], start=(c == 0), stop=(c == 1))
                    g.then_inc(s.gate, 1)
                R.taken(n, s.gate, (n + 1) * NT)
            R.taken(2, s.gate, 2 * NT)

        @block.scalar
        def _(act):
            norm_scalar(act, k, s, gain)
            for j in range(2 * NT):
                act.wait_ge(s.gate, j + 1)
                if j >= 2:
                    act.wait_ge(s.sum, j - 1)
                act.activation(k.sg[:, j % 2, :], k.bank[j % 4][:, :], ACT.Sigmoid).then_inc(s.sig, 1)

        @block.vector
        def _(dve):
            norm_vector(dve, k, s, gain)
            for j in range(2 * NT):
                n, t = j // NT, j % NT
                dve.wait_ge(s.sig, j + 1)
                dve.tensor_tensor(k.sg[:, j % 2, :], k.sg[:, j % 2, :], k.bank[4 + j % 4][:, :],
                                  ALU.mult).then_inc(s.prod, 1)
                dve.wait_ge(s.prod, j + 1)
                out = k.H[:, t, n * HALF:(n + 1) * HALF]
                dve.tensor_tensor(out, out, k.sg[:, j % 2, :], ALU.add).then_inc(s.sum, 1)

        @block.sync
        def _(sp):
            sp.dma_start(k.pT[:, :, :], k.p_t[layer].rearrange("(p c) n -> p c n", c=2)).then_inc(s.p, 16)
            if store:
                for t in range(NT):
                    sp.wait_ge(s.sum, NT + t + 1)
                    sp.dma_start(k.out_t[:, t, :], k.H[:, t, :]).then_inc(k.s_out, 16)
                sp.wait_ge(k.s_out, 16 * NT)
            following(sp)


def nc_block(k):
    return k.nc.Block()


def host_distances():
    j = np.arange(P)
    parts = []
    for d in range(4):
        dist = (4 * j[:, None] + d - np.arange(SEQ)[None, :]).astype(np.float32)
        parts.append(np.where((dist >= 0) & (dist <= WINDOW), dist, BIG))
    steps = j[:, None] - j[None, :]
    for every in (1, 4):
        parts.append(np.where((steps >= 0) & (steps % every == 0), 4.0 * steps, BIG))
    return np.concatenate(parts, axis=1).astype(np.float32)


CONSTS = (("ident", P), ("ones", P), ("before", P), ("upto", P), ("iota", P),
          ("first", EXPERTS), ("eps", 1))


def host_constants():
    i = np.arange(P)
    t = {
        "ident": np.eye(P),
        "ones": np.ones((P, P)),
        "before": (i[:, None] < i[None, :]),
        "upto": (i[:, None] <= i[None, :]),
        "eps": np.full((P, 1), EPS),
        "iota": np.broadcast_to(i[None, :], (P, P)),
        "first": np.broadcast_to(EXPERTS - np.arange(EXPERTS)[None, :], (P, EXPERTS)),
    }
    return np.concatenate([np.asarray(t[n], np.float32) for n, _ in CONSTS], axis=1)


def host_join():
    i = np.arange(P)
    return np.ascontiguousarray(np.stack(
        [((i[:, None] >> l) % 2 == 1) & ((i[:, None] >> l) == (i[None, :] >> l) + 1) for l in range(LEVELS)],
        axis=1).astype(np.float32))


def build(nc, t, out):
    with ExitStack() as ctx:
        k = Net()
        k.nc = nc
        scope = [ctx]

        def sb(name, shape, dt=F32):
            names.append(name)
            return scope[-1].enter_context(nc.sbuf_tensor(f"{name}_{len(names)}", shape, dt))

        names = []
        k.sems = []

        def sem(name):
            k.sems.append(nc.alloc_semaphore(name=name))
            return k.sems[-1]

        k.sem = sem
        k.bank = [ctx.enter_context(nc.psum_tensor(f"bank{i}", [P, HALF], F32)) for i in range(8)]
        k.w1, k.w3, k.w2, k.w_heads, k.p_t = (t[name] for name in ("w1", "w3", "w2", "w_heads", "p_t"))
        k.dist_d = t["dist"]
        k.w_gate, k.w_proj, k.w_ab_d = t["w_ple_gate"], t["w_ple_proj"], t["w_ab"]
        k.out_t = out[0].rearrange("(t p) d -> p t d", p=P)

        k.ring = sb("ring", [P, RING, 4096])
        k.H = sb("H", [P, NT, D])
        k.xnT = sb("xnT", [P, DC, SEQ])
        k.consts = sb("consts", [P, sum(n for _, n in CONSTS)])
        k.consts_b = sb("consts_b", [P, 2, P], BF16)
        ends = np.cumsum([n for _, n in CONSTS])
        k.ident, k.ones, k.before, k.upto, k.iota, k.first, k.eps = (
            k.consts[:, int(end) - n:int(end)] for (_, n), end in zip(CONSTS, ends))
        k.ones_b, k.before_b = k.consts_b[:, 0, :], k.consts_b[:, 1, :]
        k.g_a = sb("g_a", [P, DC])
        k.g_o = sb("g_o", [P, 1])
        k.g_kv = sb("g_kv", [P, DC])
        k.g_b = sb("g_b", [P, DC])
        k.g_kq = sb("g_kq", [P, 2, GROUPS])
        k.g_ffn = sb("g_ffn", [P, 2, DC])
        k.g_ple = sb("g_ple", [P, 2, DC])
        (k.ss, k.var, k.std, k.rstd) = (
            sb(name, [P, NT]) for name in
            ("ss", "var", "std", "rstd"))
        k.w_router = sb("w_router", [P, 2, DC, MG + EXPERTS])
        k.b_router = sb("b_router", [P, 2, MG + EXPERTS])
        k.extra = sb("extra", [P, 2], I32)
        k.s_out = k.sem("stored")
        s_const, s_x, s_cb = k.sem("constants"), k.sem("x"), k.sem("consts_b")
        k.R = Ring(k.ring, [k.sem(f"landed{i}") for i in range(RING)])
        kept = len(k.sems)

        def end_phase():
            nc.clear_and_free_semaphores(k.sems[kept:])
            nc.all_engine_barrier()
            del k.sems[kept:]
            k.R.free = [None] * RING

        def phase():
            st = ExitStack()
            scope.append(st)
            st.callback(scope.pop)
            return st

        with phase():
            (k.beta, k.glog, k.G, k.eG, k.eGlast, k.eGrest, k.beG, k.ax, k.sp) = (
                sb(name, [P, NT, HEADS]) for name in
                ("beta", "glog", "G", "eG", "eGlast", "eGrest", "beG", "ax", "sp"))
            k.eA = sb("eA", [P, HEADS])
            k.dt_bias = sb("dt_bias", [P, HEADS])
            k.w_ab = sb("w_ab", [P, DC, 2 * HEADS])
            k.conv_w = sb("conv_w", [P, 3, HEADS * CONV])
            k.join = sb("join", [P, LEVELS, P])

            with nc_block(k) as block:

                @block.scalar
                def _(act):
                    n = 0
                    loads = [
                        (k.consts[:, :], t["consts"]),
                        (k.conv_w[:, :, :], t["conv_w"]),
                        (k.join[:, :, :], t["join"]),
                        (k.g_a[:, :], t["a_norm"][0].rearrange("(p c) -> p c", c=DC)),
                        (k.g_o[:, :], t["a_o_norm"][0].rearrange("(p c) -> p c", c=1)),
                        (k.eA[:, :], t["a_A_log"][0:1, :].to_broadcast([P, HEADS])),
                        (k.dt_bias[:, :], t["a_dt_bias"][0:1, :].to_broadcast([P, HEADS])),
                        (k.g_kv[:, :], t["kv_norm"].rearrange("(p c) -> p c", c=DC)),
                        (k.g_b[:, :], t["b_norm"][0].rearrange("(p c) -> p c", c=DC)),
                        (k.g_kq[:, :, :], t["g_kq"]),
                        (k.g_ffn[:, :, :], t["ffn_norm"].rearrange("l (p c) -> p l c", c=DC)),
                        (k.g_ple[:, :, :], t["ple_norm"].rearrange("l (p c) -> p l c", c=DC)),
                    ]
                    for l in range(2):
                        loads += [(k.w_router[:, l, :, :], t["w_router"][l].rearrange("(p c) n -> p c n", c=DC)),
                                  (k.b_router[:, l, :], t["b_router"][l:l + 1, :].to_broadcast([P, MG + EXPERTS]))]
                    for dst, src in loads:
                        act.dma_start(dst, src).then_inc(s_const, 16)
                        n += 16
                    act.wait_ge(s_const, n)
                    act.activation(k.consts_b[:, 0, :], k.ones, ACT.Copy).then_inc(s_cb, 1)
                    act.activation(k.consts_b[:, 1, :], k.before, ACT.Copy).then_inc(s_cb, 1)

                @block.sync
                def _(sp):
                    sp.dma_start(k.H[:, :, :], t["x"][0].rearrange("(t p) d -> p t d", p=P)).then_inc(s_x, 16)
                    for h in range(2):
                        dst, src = load_head(k, h, h)
                        k.R.load(sp, h, dst, src)
                    sp.wait_ge(s_x, 16)

            w_out = t["a_w_out"][0].rearrange("(h p) n -> p h n", p=P)

            def first(sp):
                for n in range(2):
                    k.R.load(sp, 2 + n, k.R.flat(2 + n).rearrange("p (h n) -> p h n", h=HEADS),
                             w_out[:, :, n * HALF:(n + 1) * HALF])

            with phase():
                k.xn = sb("xn", [P, NT, D])
                delta_gates(k, first)
            end_phase()
            k.oT = k.R.flat(4).rearrange("p (h n) -> p h n", h=HEADS)
            k.qkvz = k.R.flat(5).rearrange("p (b j n) -> p b j n", b=2, j=4)
            with phase():
                k.cv = sb("cv", [P, 3, SEQ])
                k.sqr = sb("sqr", [P, 2, SEQ])
                k.rnorm = sb("rnorm", [P, 3, SEQ])
                (k.glogB, k.dif, k.lo, k.hi, k.kb, k.kd, k.vb, k.T, k.V, k.X, k.A, k.us) = (
                    sb(name, [P, NT, P]) for name in
                    ("glogB", "dif", "lo", "hi", "kb", "kd", "vb", "T", "V", "X", "A", "us"))
                (k.qg, k.eGrow, k.nWT, k.osq, k.og) = (
                    sb(name, [P, SEQ]) for name in
                    ("qg", "eGrow", "nWT", "osq", "og"))
                k.C = sb("C", [P, LEVELS, NT, P])
                k.state = sb("state", [P, 2, P])
                delta_heads(k, lambda sp: prefetch_experts(sp, k, 0, (0, 1)))
            end_phase()

            def halves(pe, n):
                k.R.arrived(pe, 2 + n)
                k.R.takes[2 + n] += 1
                w = k.R.flat(2 + n).rearrange("p (h n) -> p h n", h=HEADS)
                return lambda c: w[:, c, :]

            def then(sp, done):
                k.R.free[2], k.R.free[3] = (done, NT), (done, 2 * NT)
                k.R.free[4] = k.R.free[5] = (done, 2 * NT)
                prefetch_experts(sp, k, 0, (2, 3, 4, 5))

            project_out(k, "dn_out", k.oT, HEADS, halves, then)
            end_phase()

        def load_kv(sp):
            for w, slot in ((t["w_kv"], 3), (t["b_w_q"][0], 0)):
                for g in range(GROUPS):
                    k.R.load(sp, slot + g, k.R.flat(slot + g).rearrange("p (c n) -> p c n", c=DC),
                             w.rearrange("(p c) n -> p c n", c=DC)[:, :, g * HALF:(g + 1) * HALF])

        for layer in range(2):
            with phase():
                k.xn = sb("xn", [P, NT, D])
                k.xs = sb("xs", [P, 3, NT, D], BF16)
                k.lg = sb("lg", [P, NT, MG + EXPERTS])
                (k.gd, k.gq, k.ge) = (
                    sb(name, [P, NT, MG]) for name in
                    ("gd", "gq", "ge"))
                (k.gm, k.gs, k.m1, k.m2, k.ed, k.e2, k.c1, k.c2) = (
                    sb(name, [P, NT]) for name in
                    ("gm", "gs", "m1", "m2", "ed", "e2", "c1", "c2"))
                (k.el, k.eq, k.oh1, k.oh2, k.Wt, k.rank) = (
                    sb(name, [P, NT, EXPERTS]) for name in
                    ("el", "eq", "oh1", "oh2", "Wt", "rank"))
                k.M = sb("M", [P, NT, EXPERTS], BF16)
                k.most = sb("most", [P, 1])
                k.most_i = sb("most_i", [P, 1], I32)
                k.slot1h = sb("slot1h", [P, NT, 2 * SLOTS], BF16)
                k.slotw = sb("slotw", [P, NT, 2 * SLOTS])
                k.xT = sb("xT", [P, DC, 2 * SLOTS])
                k.h1s = sb("h1s", [P, FF])
                k.h = sb("h", [P, FF])
                k.hT = sb("hT", [P, FC, 2 * SLOTS])
                k.S = sb("S", [P, SEQ])
                k.y = sb("y", [P, D])
                route(k, layer, lambda sp: None)
                experts(k, layer, lambda sp: prefetch_ple(sp, k, layer))
                more_experts(k, layer, lambda sp: prefetch_ple(sp, k, layer))
            end_phase()
            with phase():
                k.xn = sb("xn", [P, NT, D])
                k.sg = sb("sg", [P, 2, HALF])
                k.pT = sb("pT", [P, 2, SEQ])
                embed(k, layer, load_kv if layer == 0 else (lambda sp: None), store=(layer == 1))
            end_phase()
            if layer == 1:
                break
            with phase():
                k.kT = sb("kT", [P, GROUPS * KVPG, SEQ])
                k.V = sb("V", [P, GROUPS, NT, KVPG * HD])
                k.qT = sb("qT", [P, GROUPS * QPG, SEQ])
                with phase():
                    k.xn = sb("xn", [P, NT, D])
                    k.sqr = sb("sqr", [P, 2, SEQ])
                    k.rnorm = sb("rnorm", [P, 2, SEQ])

                    def weights(slot, per):
                        def of(pe, j):
                            if j % per == 0:
                                k.R.arrived(pe, slot + j // per)
                            return k.R.flat(slot + j // per).rearrange("p (c n) -> p c n", c=DC)[
                                :, :, j % per * HD:(j % per + 1) * HD]
                        return of

                    def after_kv(sp):
                        k.R.load(sp, 3, k.R.flat(3).rearrange("p (h n) -> p h n", h=QPG), t["b_w_out"][0].rearrange("(h p) n -> p h n", p=P))
                        prefetch_experts(sp, k, 1, (4, 5))

                    head_features(k, "kf", k.g_kv, weights(3, KVPG), GROUPS * KVPG, k.kT, k.g_kq[:, 0, :],
                                  (3, 4, 5), after_kv, values=Values(k))
                    end_phase()
                    head_features(k, "qf", k.g_b, weights(0, QPG), GROUPS * QPG, k.qT, k.g_kq[:, 1, :],
                                  (0, 1, 2), lambda sp: prefetch_experts(sp, k, 1, (0, 1, 2)), scale=HD ** -0.5,
                                  fresh=False)
                    end_phase()
                with phase():
                    k.dist = sb("dist", [P, 4 * SEQ + 2 * P])
                    k.sc = sb("sc", [P, 2, NSCORE])
                    k.PT = sb("PT", [P, NSCORE])
                    k.aoT = k.xnT[:, 0:QPG, :]
                    (k.peak, k.total, k.inv) = (
                        sb(name, [P, 2]) for name in
                        ("peak", "total", "inv"))
                    attend(k, lambda sp: None)
                    end_phase()

                    def whole(pe, n):
                        if n == 0:
                            k.R.arrived(pe, 3)
                        w = k.R.flat(3).rearrange("p (h n) -> p h n", h=QPG)
                        return lambda c: w[:, c, n * HALF:(n + 1) * HALF]

                    def then(sp, done):
                        k.R.takes[3] += 1
                        k.R.free[3] = (done, 2 * NT)
                        prefetch_experts(sp, k, 1, (3,))

                    project_out(k, "at_out", k.aoT, QPG, whole, then)
                    end_phase()


_INS = ["x", "kv_norm", "w_kv", "b_norm", "b_w_q", "b_w_out", "a_norm", "a_A_log", "a_dt_bias", "a_o_norm", "a_w_out", "ffn_norm", "w1", "w3", "w2", "ple_norm", "w_ple_gate", "w_ple_proj"]


def kernel(**inputs):
    import numpy as _np
    import concourse.bacc as _bacc
    from concourse import mybir as _mybir
    from concourse.bass_utils import run_bass_kernel_spmd as _run

    nc = _bacc.Bacc("TRN2", target_bir_lowering=False, num_devices=1)
    data = {name: _np.ascontiguousarray(inputs[name]) for name in _INS}
    data["p_t"] = _np.ascontiguousarray(_np.asarray(inputs["p"])[:, 0].transpose(0, 2, 1))
    w_in = _np.asarray(inputs["a_w_in"])[0]
    heads = w_in[:, :4 * HEADS * DK].reshape(P, DC, 4, HEADS, DK)
    data["w_heads"] = _np.ascontiguousarray(heads.transpose(3, 0, 1, 2, 4)).reshape(HEADS, P, 4096)
    data["w_ab"] = _np.ascontiguousarray(w_in[:, 4 * HEADS * DK:])
    taps = _np.asarray(inputs["a_conv"])[0].reshape(CONV, 3, HEADS, P)
    data["conv_w"] = _np.ascontiguousarray(taps.transpose(3, 1, 2, 0)).reshape(P, 3, HEADS * CONV)
    for what in ("w", "b"):
        data[f"{what}_router"] = _np.concatenate(
            [_np.asarray(inputs[f"{what}_router_{part}"]) for part in ("group", "expert")], axis=-1)
    data["g_kq"] = _np.ascontiguousarray(
        _np.stack([_np.asarray(inputs["k_norm"]), _np.asarray(inputs["b_q_norm"])[0]]).transpose(2, 0, 1))
    data["dist"] = host_distances()
    data["consts"] = host_constants()
    data["join"] = host_join()
    arrays, aps = {}, {}
    for name, a in data.items():
        arrays[f"in_{name}"] = a
        aps[name] = nc.dram_tensor(f"in_{name}", a.shape, _mybir.dt.from_np(a.dtype), kind="ExternalInput").ap()
    out = nc.dram_tensor("out_0", (1, SEQ, D), F32, kind="ExternalOutput").ap()
    build(nc, aps, out)
    r = _run(nc, [arrays], core_ids=[0])
    return r.results[0]["out_0"]
```

```python
from contextlib import ExitStack

import concourse.bass as bass
from concourse import mybir
import numpy as np

F32 = mybir.dt.float32
BF16 = mybir.dt.bfloat16
I32 = mybir.dt.int32
ACT = mybir.ActivationFunctionType
ALU = mybir.AluOpType
AX = mybir.AxisListType

P = 128
D = 1024
SEQ = 512
NT = SEQ // P
DC = D // P
HALF = 512
EPS = 1e-6
PLE = 256
HEADS, DK = 8, 128
CONV = 4
QKV = 3 * HEADS * DK
GROUPS, QPG, KVPG, HD = 3, 4, 2, 128
DILS, WINDOW = (1, 4, 16), 128
MG, ME = 4, 8
EXPERTS = MG * ME
PAIRS = EXPERTS // 2
FF = 512
FC = FF // P
SLOTS = 64
BIG = 1e30
NOT_CHOSEN = 65536.0
RING = 6


def wait(eng, sem, value):
    if isinstance(value, int) and value <= 0:
        return
    eng.wait_ge(sem, value)


class Chain:

    def __init__(self, eng, sem, start=0):
        self.eng, self.sem, self.n, self.start = eng, sem, 0, start

    def link(self, ins):
        self.n += 1
        ins.then_inc(self.sem, 1)
        self.eng.wait_ge(self.sem, self.start + self.n)


class Ring:

    def __init__(self, buf, landed):
        self.buf, self.landed = buf, landed
        self.free, self.takes = [None] * RING, [0] * RING

    def load(self, sp, slot, dst, src):
        if self.free[slot]:
            sp.wait_ge(*self.free[slot])
        sp.dma_start(dst, src).then_inc(self.landed[slot], 16)

    def arrived(self, pe, slot, i=0):
        pe.wait_ge(self.landed[slot], (self.takes[slot] + 1 + i) * 16)

    def taken(self, slot, sem, value):
        self.takes[slot] += 1
        self.free[slot] = (sem, value)

    def flat(self, slot, n=4096):
        return self.buf[:, slot, 0:n]


class Net:
    pass


def bcast(ap, axis, n):
    shape = list(ap.shape)
    shape.insert(axis, n)
    return ap.unsqueeze(axis).to_broadcast(shape)




def load_expert_pair(k, layer, pair, load):
    for m, (w, chunks) in enumerate(((k.w1, DC), (k.w3, DC), (k.w2, FC))):
        src = w[layer].rearrange("(q e) (p c) n -> q p e (c n)", e=2, c=chunks)
        for half in range(2):
            slot = 2 * m + half
            load(slot, k.ring[:, slot, :].rearrange("p (e x) -> p e x", e=2),
                 src[bass.ds(pair, 1), :, :, half * 2048:(half + 1) * 2048].rearrange("q p e x -> (q p) e x"))


def prefetch_experts(sp, k, layer, slots=range(RING)):
    load_expert_pair(k, layer, 0, lambda slot, dst, src: k.R.load(sp, slot, dst, src) if slot in slots else None)


def prefetch_ple(sp, k, layer):
    src = k.w_gate[layer].rearrange("(p c) n -> p c n", c=DC)
    for half in range(2):
        k.R.load(sp, half, k.R.flat(half).rearrange("p (c n) -> p c n", c=DC),
                 src[:, :, half * HALF:(half + 1) * HALF])
    k.R.load(sp, 2, k.R.flat(2, 2048), k.w_proj[layer].rearrange("(p c) n -> p (c n)", c=2))




def norm_semaphores(k, tag):
    s = Net()
    (s.ss, s.ss_odd, s.var, s.std, s.rstd, s.xn, s.xn_odd, s.turned, s.xnT, s.xnT_odd) = (
        k.sem(f"{tag}_{name}") for name in
        ("ss", "ss_odd", "var", "std", "rstd", "xn", "xn_odd", "turned", "xnT", "xnT_odd"))
    return s


def norm_chunk(pe, s, c):
    pe.wait_ge(s.xnT_odd if c % 2 else s.xnT, c // 2 + 1)


def norm_scalar(act, k, s, gain, fresh=True, meanwhile=None, banks=DC):
    if fresh:
        norm_scalar_rows(act, k, s)
    if meanwhile:
        meanwhile()
    for c in range(1, DC, 2):
        act.wait_ge(s.turned, c + 1)
        act.activation(k.xnT[:, c, :], k.bank[c % banks][:, :], ACT.Copy, scale=gain[:, c:c + 1]).then_inc(s.xnT_odd, 1)


def norm_scalar_rows(act, k, s, arrived=None):
    for t in range(0, NT, 2):
        if arrived:
            act.wait_ge(arrived[t], 16)
        act.activation(k.xn[:, t, :], k.H[:, t, :], ACT.Square, accum_out=k.ss[:, t:t + 1]).then_inc(s.ss, 1)
    act.wait_ge(s.var, 1)
    act.activation(k.std[:, :], k.var[:, :], ACT.Sqrt).then_inc(s.std, 1)
    act.wait_ge(s.rstd, 1)
    for t in range(1, NT, 2):
        act.activation(k.xn[:, t, :], k.H[:, t, :], ACT.Copy, scale=k.rstd[:, t:t + 1]).then_inc(s.xn_odd, 1)


def load_sqrt_table(act, k):
    act.activation(k.scrap[:, :], k.eps, ACT.Sqrt)


def norm_vector(dve, k, s, gain, fresh=True, banks=DC):
    if fresh:
        norm_vector_rows(dve, k, s)
    for c in range(0, DC, 2):
        dve.wait_ge(s.turned, c + 1)
        dve.tensor_scalar(k.xnT[:, c, :], k.bank[c % banks][:, :], gain[:, c:c + 1], None,
                          ALU.mult).then_inc(s.xnT, 1)


def norm_vector_rows(dve, k, s, arrived=None):
    for t in range(1, NT, 2):
        if arrived:
            dve.wait_ge(arrived[t], 16)
        dve.tensor_tensor_reduce(k.xn[:, t, :], k.H[:, t, :], k.H[:, t, :], 1.0, 0.0, ALU.mult, ALU.add,
                                 accum_out=k.ss[:, t:t + 1]).then_inc(s.ss_odd, 1)
    dve.wait_ge(s.ss_odd, NT // 2)
    dve.wait_ge(s.ss, NT // 2)
    dve.tensor_scalar(k.var[:, :], k.ss[:, :], 1.0 / D, EPS, ALU.mult, ALU.add).then_inc(s.var, 1)
    dve.wait_ge(s.std, 1)
    dve.reciprocal(k.rstd[:, :], k.std[:, :]).then_inc(s.rstd, 1)
    dve.wait_ge(s.rstd, 1)
    for t in range(0, NT, 2):
        dve.tensor_scalar(k.xn[:, t, :], k.H[:, t, :], k.rstd[:, t:t + 1], None, ALU.mult).then_inc(s.xn, 1)


def norm_tensor(pe, k, s, fresh=True, chunks=range(DC), banks=DC):
    for t in range(NT):
        if fresh:
            pe.wait_ge(s.xn_odd if t % 2 else s.xn, t // 2 + 1)
        for c in chunks:
            if t == 0 and c >= banks:
                norm_chunk(pe, s, c - banks)
            last = pe.transpose(k.bank[c % banks][:, t * P:(t + 1) * P], k.xn[:, t, c::DC], k.ident)
            if t == NT - 1:
                last.then_inc(s.turned, 1)




def gate_semaphores(k):
    g = norm_semaphores(k, "dg")
    g.x = [k.sem(f"dg_x{t}") for t in range(NT)]
    (g.early, g.late, g.cb, g.ab, g.eb, g.shifted, g.es, g.ln, g.eA, g.glog, g.sums, g.eG, g.diff, g.steps,
     g.acts) = (
        k.sem(f"dg_{name}") for name in
        ("early", "late", "cb", "ab", "eb", "shifted", "es", "ln", "eA", "glog", "sums", "eG", "diff", "steps",
         "acts"))
    return g


def gates_tensor(pe, k, g):
    pe.wait_ge(g.early, k.n_early)
    norm_tensor(pe, k, g)
    norm_chunk(pe, g, DC - 2)
    norm_chunk(pe, g, DC - 1)
    for t in range(NT):
        for c in range(DC):
            last = pe.matmul(k.bank[2][:, t * 2 * HEADS:(t + 1) * 2 * HEADS], k.xnT[:, c, t * P:(t + 1) * P],
                             k.w_ab[:, c, :], start=(c == 0), stop=(c == DC - 1))
    last.then_inc(g.ab, 1)


def gates_sums(pe, k, g):
    pe.wait_ge(g.glog, 1)
    glog = k.glog[:, :, :].rearrange("p t h -> p (t h)")
    pe.matmul(k.bank[3][:, 0:NT * HEADS], k.upto, glog, start=True, stop=True)
    pe.matmul(k.bank[3][:, NT * HEADS:2 * NT * HEADS], k.ones, glog, start=True, stop=True).then_inc(g.sums, 1)


def gates_scalar(act, k, g):
    norm_scalar_rows(act, k, g, g.x)
    act.wait_ge(g.early, k.n_early)
    norm_scalar(act, k, g, k.g_a, fresh=False)
    act.activation(k.consts_b[:, 0, :], k.ones, ACT.Copy).then_inc(g.cb, 1)
    act.activation(k.consts_b[:, 1, :], k.before, ACT.Copy).then_inc(g.cb, 1)
    ab = k.bank[2][:, 0:NT * 2 * HEADS].rearrange("p (t h) -> p t h", t=NT)
    act.activation(k.eA[:, :], k.eA[:, :], ACT.Exp).then_inc(g.eA, 1)
    act.wait_ge(g.shifted, 1)
    act.activation(k.beta[:, :, :], ab[:, :, 0:HEADS], ACT.Exp, scale=-1.0).then_inc(g.eb, 1)
    act.activation(k.sp[:, :, :], k.sp[:, :, :], ACT.Exp, scale=-1.0).then_inc(g.es, 1)
    act.wait_ge(g.es, 1)
    act.activation(k.sp[:, :, :], k.sp[:, :, :], ACT.Ln, bias=1.0).then_inc(g.ln, 1)
    act.wait_ge(g.sums, 1)
    act.activation(k.eG[:, :, :].rearrange("p t h -> p (t h)"), k.bank[3][:, 0:NT * HEADS],
                   ACT.Exp).then_inc(g.eG, 1)
    act.activation(k.eGlast[:, :, :].rearrange("p t h -> p (t h)"), k.bank[3][:, NT * HEADS:2 * NT * HEADS],
                   ACT.Exp).then_inc(g.acts, 1)
    act.wait_ge(g.diff, 1)
    act.activation(k.eGrest[:, :, :], k.eGrest[:, :, :], ACT.Exp).then_inc(g.acts, 1)


def gates_vector(dve, k, g):
    norm_vector_rows(dve, k, g, g.x)
    dve.wait_ge(g.early, k.n_early)
    norm_vector(dve, k, g, k.g_a, fresh=False)
    ch = g.chain = Chain(dve, g.steps)
    ab = k.bank[2][:, 0:NT * 2 * HEADS].rearrange("p (t h) -> p t h", t=NT)
    dve.wait_ge(g.ab, 1)
    ch.link(dve.tensor_tensor(k.ax[:, :, :], ab[:, :, HEADS:], bcast(k.dt_bias[:, :], 1, NT), ALU.add))
    ch.link(dve.tensor_scalar(k.sp[:, :, :], k.ax[:, :, :], -1.0, None, ALU.mult))
    dve.tensor_tensor(k.sp[:, :, :], k.sp[:, :, :], k.ax[:, :, :], ALU.max).then_inc(g.shifted, 1)
    dve.wait_ge(g.eb, 1)
    ch.link(dve.tensor_scalar(k.beta[:, :, :], k.beta[:, :, :], 1.0, None, ALU.add))
    ch.link(dve.reciprocal(k.beta[:, :, :], k.beta[:, :, :]))
    dve.wait_ge(g.ln, 1)
    ch.link(dve.scalar_tensor_tensor(k.ax[:, :, :], k.ax[:, :, :], 0.0, k.sp[:, :, :], ALU.max, ALU.add))
    dve.wait_ge(g.eA, 1)
    dve.scalar_tensor_tensor(k.glog[:, :, :], k.ax[:, :, :], -1.0, bcast(k.eA[:, :], 1, NT), ALU.mult,
                             ALU.mult).then_inc(g.glog, 1)


def gates_vector_sums(dve, k, g):
    ch = g.chain
    dve.wait_ge(g.acts, 1)
    G = k.G[:, :, :].rearrange("p t h -> p (t h)")
    ch.link(dve.tensor_copy(G, k.bank[3][:, 0:NT * HEADS]))
    dve.tensor_tensor(k.eGrest[:, :, :].rearrange("p t h -> p (t h)"),
                      k.bank[3][:, NT * HEADS:2 * NT * HEADS], G, ALU.subtract).then_inc(g.diff, 1)
    ch.link(dve.tensor_tensor(k.beG[:, :, :], k.beta[:, :, :], k.eG[:, :, :], ALU.mult))
    dve.wait_ge(g.acts, 2)


def load_head(k, h, slot):
    return k.ring[:, slot, :], k.w_heads[bass.ds(h, 1), :, :].rearrange("h p x -> (h p) x")


def head_of(ap, h):
    return ap[:, :, bass.ds(h, 1)].rearrange("p t h -> p (t h)")


LEVELS = P.bit_length() - 1


OUT_BANKS = (0, 2, 1, 5, 6, 3, 4, 7)
EARLY = 6


def delta(k, loads, following):
    g = gate_semaphores(k)
    s = Net()
    done, added = k.sem("dn_done"), k.sem("dn_added")
    (s.proj, s.ssq, s.grams, s.turned, s.Vt, s.X, s.Y, s.Z, s.W, s.u, s.o, s.dS, s.oss, s.sil, s.sq, s.ln,
     s.rn, s.dec, s.eg, s.Xs, s.V0, s.nW, s.us, s.osq, s.conv, s.cstep, s.qkn, s.gB, s.clip, s.L, s.A, s.T0,
     s.Vs, s.Ts, s.v_turned, s.tok, s.qg, s.St, s.og, s.vstep, s.C) = (
        k.sem(f"dn_{name}") for name in (
            "proj", "ssq", "grams", "turned", "Vt", "X", "Y", "Z", "W", "u", "o", "dS", "oss", "sil", "sq",
            "ln", "rn", "dec", "eg", "Xs", "V0", "nW", "us", "osq", "conv", "cstep", "qkn", "gB", "clip",
            "L", "A", "T0", "Vs", "Ts", "v_turned", "tok", "qg", "St", "og", "vstep", "C"))
    R = k.R
    bank = k.bank
    nl = LEVELS - 1
    tile = lambda a, t: a[:, t * P:(t + 1) * P]
    four = lambda a: a.rearrange("p (t n) -> p t n", t=NT)

    def blocks(a, l, odd):
        if len(a.shape) == 3:
            a = a.rearrange("p t n -> p (t n)")
        return a.rearrange("p (n two b) -> p n two b", two=2, b=1 << l)[:, :, odd, :]

    with nc_block(k) as block:

        @block.tensor
        def _(pe):
            def projection(h, par):
                pe.wait_ge(R.landed[par], h * 8 + (16 * (R.takes[par] + 1) - 8 * par))
                w = R.flat(par).rearrange("p (c j n) -> p c j n", c=DC, j=4)
                for j in range(4):
                    if j == 0:
                        wait(pe, s.conv, 3 * h)
                    elif j == 1:
                        wait(pe, s.sil, 4 * h)
                    else:
                        pe.wait_ge(s.conv, 3 * h + j - 1)
                    for c in range(DC):
                        m = pe.matmul(bank[j % 2][:, :], w[:, c, j, :], k.xnT[:, c, :], start=(c == 0),
                                      stop=(c == DC - 1))
                        if c == DC - 1:
                            m.then_inc(s.proj, 1)
                        yield

            def norm_sums(h, j, par):
                pe.wait_ge(s.sq, 2 * h + j + 1)
                pe.matmul(bank[(2, 5)[j]][:, :], k.ones, k.sqr[:, j, :], start=True, stop=True).then_inc(s.ssq, 1)

            def head(h, par, follow=True):
                q, kk, v = (k.qkvz[:, par, j, :] for j in range(3))
                rest = projection(h + 1, 1 - par) if follow else early_units()

                def gap(n):
                    for _ in range(n):
                        next(rest, None)

                pe.wait_ge(s.qkn, 2 * h + 2)
                pe.wait_ge(s.gB, h + 1)
                for t in range(NT):
                    pe.matmul(tile(bank[5], t), k.glogB[:, t, :], k.upto, start=True, stop=True)
                for t in range(NT):
                    pe.matmul(tile(bank[3], t), tile(kk, t), tile(kk, t), start=True, stop=True)
                for t in range(NT):
                    last = pe.matmul(tile(bank[4], t), tile(kk, t), tile(q, t), start=True, stop=True)
                last.then_inc(s.grams, 1)
                for t in range(NT):
                    last = pe.transpose(tile(bank[6], t), tile(kk, t), k.ident)
                last.then_inc(s.turned, 1)
                gap(6)
                pe.wait_ge(s.T0, h + 1)
                for t in range(NT):
                    last = pe.transpose(tile(bank[3], t), k.T[:, t, :], k.ident)
                last.then_inc(s.Vt, 1)
                gap(1)
                for l in range(1, LEVELS):
                    pe.wait_ge(s.C, nl * h + l)
                    if l == 1:
                        pe.wait_ge(s.V0, h + 1)
                    else:
                        pe.wait_ge(s.Vs, nl * h + l - 1)
                    for t in range(NT):
                        last = pe.matmul(tile(bank[3], t), k.C[:, l, t, :], k.V[:, t, :], start=True, stop=True)
                    last.then_inc(s.X, 1)
                    if l > 1:
                        for t in range(NT):
                            last = pe.transpose(tile(bank[5], t), k.V[:, t, :], k.ident)
                        last.then_inc(s.Z, 1)
                    gap(1)
                    pe.wait_ge(s.Xs, nl * h + l)
                    if l == 1:
                        pe.wait_ge(s.A, h + 1)
                        pe.wait_ge(s.eg, h + 1)
                    else:
                        pe.wait_ge(s.Ts, (nl - 1) * h + l - 1)
                    for t in range(NT):
                        last = pe.matmul(tile(bank[4], t), k.T[:, t, :], k.X[:, t, :], start=True, stop=True)
                    last.then_inc(s.Y, 1)
                    gap(1)
                    if l == 2:
                        pe.wait_ge(s.sil, 4 * h + 3)
                        wait(pe, s.og, h)
                        for t in range(NT):
                            last = pe.transpose(tile(bank[7], t), tile(v, t), k.ident)
                        last.then_inc(s.v_turned, 1)
                pe.wait_ge(s.tok, 3 * h + 3)
                pe.wait_ge(s.Vs, nl * h + nl)
                for t in range(NT):
                    last = pe.matmul(tile(bank[6], t), k.kb[:, t, :], k.V[:, t, :], start=True, stop=True)
                last.then_inc(s.W, 1)
                if follow:
                    norm_sums(h + 1, 0, 1 - par)
                for t in range(NT):
                    last = pe.matmul(tile(bank[3], t), k.V[:, t, :], k.vb[:, t, :], start=True, stop=(t == 0),
                                     skip_group_check=True)
                    if t:
                        pe.wait_ge(s.nW, h + 1)
                        pe.wait_ge(s.St, 3 * h + t)
                        last = pe.matmul(tile(bank[3], t), tile(k.nWT[:, :], t), k.state[:, (t - 1) % 2, :],
                                         start=False, stop=True, skip_group_check=True)
                    last.then_inc(s.u, 1)
                    gap(1)
                    pe.wait_ge(s.us, 4 * h + t + 1)
                    if t < NT - 1:
                        pe.matmul(tile(bank[4], t), k.kd[:, t, :], k.us[:, t, :], start=True,
                                  stop=True).then_inc(s.dS, 1)
                    if t == 0:
                        pe.wait_ge(s.qg, h + 1)
                        pe.wait_ge(s.A, h + 1)
                    else:
                        pe.matmul(tile(bank[7], t), k.state[:, (t - 1) % 2, :], tile(k.qg[:, :], t), start=True,
                                  stop=False, skip_group_check=True)
                    last = pe.matmul(tile(bank[7], t), k.us[:, t, :], k.A[:, t, :], start=(t == 0), stop=True,
                                     skip_group_check=True)
                    if t == NT - 1:
                        last.then_inc(s.o, 1)
                    gap(1)
                    if follow and t == 1:
                        pe.wait_ge(s.Ts, (nl - 1) * (h + 1))
                        norm_sums(h + 1, 1, 1 - par)
                gap(1)
                pe.wait_ge(s.osq, h + 1)
                pe.matmul(bank[4][:, :], k.ones, k.osq[:, :], start=True, stop=True).then_inc(s.oss, 1)
                for _ in rest:
                    pass

            def unit(u, chunks):
                n, t = u // NT, u % NT
                w = R.flat(2 + n).rearrange("p (h n) -> p h n", h=HEADS)
                for c in chunks:
                    yield pe.matmul(bank[OUT_BANKS[u]][:, :], k.oT[:, c, t * P:(t + 1) * P], w[:, c, :],
                                    start=(c == 0), stop=(c == HEADS - 1), skip_group_check=True)

            def early_units():
                pe.wait_ge(s.og, HEADS - 1)
                read = ((s.conv, 3 * HEADS), (s.qkn, 2 * HEADS), (s.sil, 4 * HEADS), (s.Ts, (nl - 1) * HEADS),
                        (s.nW, HEADS), (s.us, NT * HEADS))
                for u in range(EARLY):
                    pe.wait_ge(*read[u])
                    if u % NT == 0:
                        R.arrived(pe, 2 + u // NT)
                    yield from unit(u, range(HEADS - 1))

            gates_tensor(pe, k, g)
            first = projection(0, 0)
            for _ in range(2 * DC):
                next(first)
            gates_sums(pe, k, g)
            for _ in first:
                pass
            norm_sums(0, 0, 0)
            norm_sums(0, 1, 0)
            head(0, 0)
            head(1, 1)
            with pe.Fori(1, HEADS // 2 - 1) as i:
                head(2 * i, 0)
                head(2 * i + 1, 1)
            head(HEADS - 2, 0)
            head(HEADS - 1, 1, follow=False)
            pe.wait_ge(s.og, HEADS)
            for u in range(2 * NT):
                for last in unit(u, (HEADS - 1,) if u < EARLY else range(HEADS)):
                    pass
                last.then_inc(done, 1)
            for slot in range(2):
                R.takes[slot] += HEADS // 2
                R.free[slot] = (s.proj, 4 * HEADS)
                R.takes[2 + slot] += 1
                R.free[2 + slot] = (done, NT * (slot + 1))
            R.free[4] = R.free[5] = (done, 2 * NT)

        @block.vector
        def _(dve):
            def conv(h, j, par):
                x, out = bank[j % 2], k.cv[:, j, :]
                tap = lambda n: k.conv_w[:, j, bass.ds(h * CONV + n, 1)]
                dve.wait_ge(s.proj, 4 * h + j + 1)
                base = 9 * h + 3 * j
                dve.tensor_scalar(out, x[:, :], tap(CONV - 1), None, ALU.mult).then_inc(s.cstep, 1)
                yield
                for n in range(1, CONV):
                    dve.wait_ge(s.cstep, base + n)
                    ins = dve.scalar_tensor_tensor(out[:, n:], x[:, 0:SEQ - n], tap(CONV - 1 - n), out[:, n:],
                                                   ALU.mult, ALU.add)
                    ins.then_inc(s.conv if n == CONV - 1 else s.cstep, 1)
                    yield

            def steps(conv, n=CONV):
                for _ in range(n):
                    next(conv)

            def normalise(h, j, par):
                dve.wait_ge(s.rn, j + 1 if isinstance(h, int) and h == 0 else 3 * h + j)
                a = k.qkvz[:, par, j, :]
                if j == 0:
                    dve.scalar_tensor_tensor(a, a, DK ** -0.5, k.rnorm[:, 0, :], ALU.mult,
                                             ALU.mult).then_inc(s.qkn, 1)
                else:
                    dve.tensor_tensor(a, a, k.rnorm[:, 1, :], ALU.mult).then_inc(s.qkn, 1)

            def decays(h):
                dve.tensor_copy(k.glogB[:, :, :], bcast(head_of(k.glog, h), 2, P)).then_inc(s.gB, 1)

            def head(h, par, follow=True):
                q = k.qkvz[:, par, 0, :]
                n = 0
                vbase = VSTEPS * h

                def link(ins):
                    nonlocal n
                    n += 1
                    ins.then_inc(s.vstep, 1)
                    dve.wait_ge(s.vstep, vbase + n)

                dve.wait_ge(s.grams, h + 1)
                link(dve.tensor_tensor(k.dif[:, :, :], four(bank[5][:, :]), bcast(head_of(k.G, h), 2, P),
                                       ALU.subtract))
                dve.tensor_scalar(k.lo[:, :, :], k.dif[:, :, :], 0.0, None, ALU.max).then_inc(s.clip, 1)
                dve.tensor_scalar(k.hi[:, :, :], k.dif[:, :, :], 0.0, None, ALU.min).then_inc(s.clip, 1)
                dve.wait_ge(s.turned, h + 1)
                dve.tensor_tensor(k.kb[:, :, :], four(bank[6][:, :]), bcast(head_of(k.beG, h), 2, P),
                                  ALU.mult).then_inc(s.tok, 1)
                dve.wait_ge(s.dec, 2 * h + 1)
                link(dve.tensor_tensor(k.lo[:, :, :], k.lo[:, :, :], four(bank[3][:, :]), ALU.mult))
                dve.tensor_tensor(k.lo[:, :, :], k.lo[:, :, :], bcast(head_of(k.beta, h), 2, P),
                                  ALU.mult).then_inc(s.L, 1)
                dve.wait_ge(s.L, h + 1)
                link(dve.tensor_tensor(k.C[:, 0, :, :], k.lo[:, :, :], bcast(k.join[:, 0, :], 1, NT), ALU.mult))
                dve.scalar_tensor_tensor(k.T[:, :, :], k.C[:, 0, :, :], -1.0, bcast(k.ident, 1, NT), ALU.mult,
                                         ALU.add).then_inc(s.T0, 1)
                dve.wait_ge(s.dec, 2 * h + 2)
                link(dve.tensor_tensor(k.A[:, :, :], k.hi[:, :, :], four(bank[4][:, :]), ALU.mult))
                dve.tensor_tensor(k.A[:, :, :], k.A[:, :, :], bcast(k.upto, 1, NT), ALU.mult).then_inc(s.A, 1)
                dve.tensor_tensor(k.kd[:, :, :], four(bank[6][:, :]), bcast(head_of(k.eGrest, h), 2, P),
                                  ALU.mult).then_inc(s.tok, 1)
                dve.wait_ge(s.eg, h + 1)
                dve.tensor_tensor(k.qg[:, :], q, k.eGrow[:, :], ALU.mult).then_inc(s.qg, 1)
                for l in range(1, LEVELS):
                    dve.wait_ge(s.Y, nl * h + l)
                    if l > 1:
                        dve.wait_ge(s.Vs, nl * h + l - 1)
                    V = blocks(k.V[:, :, :], l, 1)
                    dve.tensor_tensor(V, V, blocks(bank[4], l, 1), ALU.subtract).then_inc(s.Vs, 1)
                    if l < nl:
                        dve.wait_ge(s.Z, (nl - 1) * h + l)
                        dve.wait_ge(s.Ts, (nl - 1) * h + l - 1) if l > 1 else None
                        T = blocks(k.T[:, :, :], l, 0)
                        dve.tensor_copy(T, blocks(bank[5], l, 0)).then_inc(s.Ts, 1)
                    if follow and l in (1, 2):
                        if l == 1:
                            of_q = conv(h + 1, 0, 1 - par)
                        steps(of_q, CONV // 2)
                    if l == 3:
                        dve.wait_ge(s.v_turned, h + 1)
                        dve.tensor_tensor(k.vb[:, :, :], four(bank[7][:, :]), bcast(head_of(k.beta, h), 2, P),
                                          ALU.mult).then_inc(s.tok, 1)
                    if follow and l == 4:
                        decays(h + 1)
                    if follow and l in (5, 6):
                        if l == 5:
                            of_k = conv(h + 1, 1, 1 - par)
                        steps(of_k, CONV // 2)
                for t in range(NT - 1):
                    dve.wait_ge(s.dS, 3 * h + t + 1)
                    new, old = k.state[:, t % 2, :], k.state[:, (t - 1) % 2, :]
                    if t == 0:
                        dve.tensor_copy(new, tile(bank[4], 0)).then_inc(s.St, 1)
                    else:
                        dve.wait_ge(s.St, 3 * h + t)
                        dve.scalar_tensor_tensor(new, old, head_of(k.eGlast, h)[:, t:t + 1], tile(bank[4], t),
                                                 ALU.mult, ALU.add).then_inc(s.St, 1)
                    if follow and t == NT - 2:
                        steps(conv(h + 1, 2, 1 - par))
                if follow:
                    normalise(h + 1, 0, 1 - par)
                    normalise(h + 1, 1, 1 - par)
                dve.wait_ge(s.rn, 3 * h + 3 + (2 if follow else 0))
                link(dve.scalar_tensor_tensor(k.og[:, :], bank[7][:, :], k.g_o[:, 0:1], k.rnorm[:, 2, :], ALU.mult,
                                              ALU.mult))
                dve.wait_ge(s.sil, 4 * h + 4)
                dve.tensor_tensor(k.oT[:, bass.ds(h, 1), :].rearrange("p h n -> p (h n)"), k.og[:, :],
                                  k.qkvz[:, par, 3, :], ALU.mult).then_inc(s.og, 1)
                assert n == VSTEPS

            VSTEPS = 5
            gates_vector(dve, k, g)
            dve.wait_ge(g.late, k.n_late)
            steps(conv(0, 0, 0))
            gates_vector_sums(dve, k, g)
            decays(0)
            steps(conv(0, 1, 0))
            steps(conv(0, 2, 0))
            normalise(0, 0, 0)
            normalise(0, 1, 0)
            head(0, 0)
            head(1, 1)
            with dve.Fori(1, HEADS // 2 - 1) as i:
                head(2 * i, 0)
                head(2 * i + 1, 1)
            head(HEADS - 2, 0)
            head(HEADS - 1, 1, follow=False)
            for u in range(2 * NT):
                dve.wait_ge(done, u + 1)
                out = k.H[:, u % NT, u // NT * HALF:(u // NT + 1) * HALF]
                dve.tensor_tensor(out, out, bank[OUT_BANKS[u]][:, :], ALU.add).then_inc(added, 1)

        @block.scalar
        def _(act):
            def silu(h, j, par):
                if j < 3:
                    act.wait_ge(s.conv, 3 * h + j + 1)
                    src = k.cv[:, j, :]
                else:
                    act.wait_ge(s.proj, 4 * h + 4)
                    src = bank[1][:, :]
                act.activation(k.qkvz[:, par, j, :], src, ACT.Silu).then_inc(s.sil, 1)
                if j < 2:
                    act.wait_ge(s.sil, 4 * h + j + 1)
                    act.activation(k.sqr[:, j, :], k.qkvz[:, par, j, :], ACT.Square).then_inc(s.sq, 1)

            def logs(h, which, count):
                for j in which:
                    if j == 2:
                        act.wait_ge(s.oss, h + 1)
                        act.activation(k.rnorm[:, 2, :], bank[4][:, :], ACT.Ln, bias=k.eps[:, 0:1],
                                       scale=1.0 / DK).then_inc(s.ln, 1)
                    else:
                        act.wait_ge(s.ssq, 2 * (h + 1) + j + 1 if count else j + 1)
                        act.activation(k.rnorm[:, j, :], bank[(2, 5)[j]][:, :], ACT.Ln,
                                       bias=k.eps[:, 0:1]).then_inc(s.ln, 1)

            def exps(h, which, done):
                act.wait_ge(s.ln, done)
                for j in which:
                    act.activation(k.rnorm[:, j, :], k.rnorm[:, j, :], ACT.Exp, scale=-0.5).then_inc(s.rn, 1)

            def head(h, par, follow=True):
                act.wait_ge(s.clip, 2 * h + 1)
                act.activation(k.lo[:, :, :], k.lo[:, :, :], ACT.Exp, scale=-1.0).then_inc(s.dec, 1)
                act.wait_ge(s.clip, 2 * h + 2)
                act.activation(k.hi[:, :, :], k.hi[:, :, :], ACT.Exp).then_inc(s.dec, 1)
                act.activation(k.eGrow[:, :], bank[5][:, :], ACT.Exp).then_inc(s.eg, 1)
                act.wait_ge(s.Vt, h + 1)
                act.activation(k.V[:, :, :], four(bank[3][:, :]), ACT.Copy).then_inc(s.V0, 1)
                for l in range(1, LEVELS):
                    act.wait_ge(s.X, nl * h + l)
                    act.activation(k.X[:, :, :], four(bank[3][:, :]), ACT.Copy).then_inc(s.Xs, 1)
                    if l == 1:
                        silu(h, 2, par)
                        silu(h, 3, par)
                    if follow and l == 3:
                        silu(h + 1, 0, 1 - par)
                act.wait_ge(s.W, h + 1)
                act.activation(k.nWT[:, :], bank[6][:, :], ACT.Copy, scale=-1.0).then_inc(s.nW, 1)
                if follow:
                    silu(h + 1, 1, 1 - par)
                for t in range(NT):
                    act.wait_ge(s.u, 4 * h + t + 1)
                    act.activation(k.us[:, t, :], tile(bank[3], t), ACT.Copy).then_inc(s.us, 1)
                act.wait_ge(s.o, h + 1)
                act.activation(k.osq[:, :], bank[7][:, :], ACT.Square).then_inc(s.osq, 1)
                if follow:
                    logs(h, (0, 1, 2), True)
                    exps(h, (0, 1, 2), 3 * h + 5)
                else:
                    logs(h, (2,), True)
                    exps(h, (2,), 3 * h + 3)

            gates_scalar(act, k, g)
            silu(0, 0, 0)
            silu(0, 1, 0)
            logs(0, (0, 1), False)
            exps(0, (0, 1), 2)
            head(0, 0)
            head(1, 1)
            with act.Fori(1, HEADS // 2 - 1) as i:
                head(2 * i, 0)
                head(2 * i + 1, 1)
            head(HEADS - 2, 0)
            head(HEADS - 1, 1, follow=False)
            load_sqrt_table(act, k)

        @block.gpsimd
        def _(pool):
            def head(h):
                pool.wait_ge(s.L, h + 1)
                for l in range(1, LEVELS):
                    pool.tensor_tensor(k.C[:, l, :, :], k.lo[:, :, :], bcast(k.join[:, l, :], 1, NT),
                                       ALU.mult).then_inc(s.C, 1)

            head(0)
            with pool.Fori(1, HEADS) as h:
                head(h)

        @block.sync
        def _(sp):
            loads(sp, g)

            def load(h, slot):
                sp.wait_ge(s.proj, 4 * (h - 1))
                dst, src = load_head(k, h, slot)
                sp.dma_start(dst, src).then_inc(R.landed[slot], 16)

            with sp.Fori(1, HEADS // 2) as i:
                load(2 * i, 0)
                load(2 * i + 1, 1)
            following(sp)


def project_out(k, tag, xT, chunks, slots_of, following):
    done, added = k.sem(f"{tag}_done"), k.sem(f"{tag}_added")
    with nc_block(k) as block:

        @block.tensor
        def _(pe):
            for n in range(2):
                w = slots_of(pe, n)
                for t in range(NT):
                    for c in range(chunks):
                        last = pe.matmul(k.bank[n * NT + t][:, :], xT[:, c, t * P:(t + 1) * P], w(c), start=(c == 0),
                                         stop=(c == chunks - 1))
                    last.then_inc(done, 1)

        @block.vector
        def _(dve):
            for j in range(2 * NT):
                dve.wait_ge(done, j + 1)
                out = k.H[:, j % NT, j // NT * HALF:(j // NT + 1) * HALF]
                dve.tensor_tensor(out, out, k.bank[j][:, :], ALU.add).then_inc(added, 1)

        @block.sync
        def _(sp):
            following(sp, done)



NSCORE = SEQ + 2 * P
NDIST = 3 + SEQ + 2 * P


def head_features(k, tag, gain, w_of, ntiles, out, norm_gain, first_slots, following, values=None, scale=None,
                  fresh=True):
    s = norm_semaphores(k, tag)
    (s.proj, s.sq, s.sums, s.ln, s.rn, s.out, s.scaled, s.vproj, s.v) = (
        k.sem(f"{tag}_{name}") for name in
        ("proj", "sq", "sums", "ln", "rn", "out", "scaled", "vproj", "v"))
    bank = k.bank
    with nc_block(k) as block:

        @block.tensor
        def _(pe):
            norm_tensor(pe, k, s, fresh)

            def sums(j):
                pe.wait_ge(s.sq, j + 1)
                if j >= 2:
                    pe.wait_ge(s.ln, j - 1)
                pe.matmul(bank[4 + j % 2][:, :], k.ones, k.sqr[:, j % 2, :], start=True, stop=True).then_inc(s.sums, 1)

            for j in range(ntiles):
                w = w_of(pe, j)
                if j >= 4:
                    pe.wait_ge(s.out, j - 3)
                for c in range(DC):
                    if j == 0:
                        norm_chunk(pe, s, c)
                    last = pe.matmul(bank[j % 4][:, :], w[:, c, :], k.xnT[:, c, :], start=(c == 0),
                                     stop=(c == DC - 1))
                last.then_inc(s.proj, 1)
                if j:
                    sums(j - 1)
            sums(ntiles - 1)
            if values:
                values.tensor(pe, s)
            for n, slot in enumerate(first_slots):
                k.R.takes[slot] += 1
                if values:
                    k.R.free[slot] = (s.vproj, (n + 1) * NT)
                else:
                    k.R.free[slot] = (s.proj, (n + 1) * QPG)

        @block.scalar
        def _(act):
            norm_scalar(act, k, s, gain, fresh)

            def root(j):
                act.wait_ge(s.sums, j + 1)
                if j >= 2:
                    act.wait_ge(s.out, j - 1)
                act.activation(k.rnorm[:, j % 2, :], bank[4 + j % 2][:, :], ACT.Ln, bias=k.eps,
                               scale=1.0 / HD).then_inc(s.ln, 1)
                act.wait_ge(s.ln, j + 1)
                act.activation(k.rnorm[:, j % 2, :], k.rnorm[:, j % 2, :], ACT.Exp, scale=-0.5).then_inc(s.rn, 1)

            for j in range(ntiles):
                act.wait_ge(s.proj, j + 1)
                if j >= 2:
                    act.wait_ge(s.sums, j - 1)
                act.activation(k.sqr[:, j % 2, :], bank[j % 4][:, :], ACT.Square).then_inc(s.sq, 1)
                if j:
                    root(j - 1)
            root(ntiles - 1)

        @block.vector
        def _(dve):
            norm_vector(dve, k, s, gain, fresh)
            if scale:
                dve.tensor_scalar(norm_gain, norm_gain, scale, None, ALU.mult).then_inc(s.scaled, 1)
                dve.wait_ge(s.scaled, 1)
            for j in range(ntiles):
                g = j * GROUPS // ntiles
                dve.wait_ge(s.rn, j + 1)
                dve.scalar_tensor_tensor(out[:, j, :], bank[j % 4][:, :], norm_gain[:, g:g + 1],
                                         k.rnorm[:, j % 2, :], ALU.mult, ALU.mult).then_inc(s.out, 1)
            if values:
                values.vector(dve, s)

        @block.sync
        def _(sp):
            following(sp)


class Values:

    def __init__(self, k):
        self.k = k

    def tensor(self, pe, s):
        k = self.k
        for g in range(GROUPS):
            w = k.R.flat(3 + g).rearrange("p (c n) -> p c n", c=DC)[:, :, KVPG * HD:]
            for d in range(NT):
                n = g * NT + d
                if n >= 2:
                    pe.wait_ge(s.v, n - 1)
                for c in range(DC):
                    x = k.xnT[:, c, d * P:(d + 1) * P] if g == 0 else k.xnT[:, c, d::4]
                    last = pe.matmul(k.bank[6 + n % 2][:, 0:KVPG * HD], x, w[:, c, :], start=(c == 0),
                                     stop=(c == DC - 1))
                last.then_inc(s.vproj, 1)

    def vector(self, dve, s):
        k = self.k
        for n in range(GROUPS * NT):
            dve.wait_ge(s.vproj, n + 1)
            dve.tensor_copy(k.V[:, n // NT, n % NT, :], k.bank[6 + n % 2][:, 0:KVPG * HD]).then_inc(s.v, 1)


def attend(k, following):
    s = Net()
    (s.S, s.biased, s.peak, s.exp, s.inv, s.prob, s.turned, s.PTa, s.PTb, s.O, s.out) = (
        k.sem(f"at_{name}") for name in
        ("S", "biased", "peak", "exp", "inv", "prob", "turned", "PTa", "PTb", "O", "out"))
    bank = k.bank
    blocks = [(qh, d) for qh in range(QPG) for d in range(4)]
    NB = len(blocks)
    slope = lambda g, qh: 2.0 ** (-8.0 * (g * QPG + qh + 1) / (GROUPS * QPG))
    with nc_block(k) as block:

        @block.tensor
        def _(pe):
            def scores(b):
                qh, d = blocks[b]
                kv = qh // 2
                if b >= 2:
                    pe.wait_ge(s.biased, 2 * (b - 1))
                pe.matmul(bank[b % 2][:, :], k.qT[:, qh, d::4], k.kT[:, kv, :], start=True, stop=True)
                for g in (1, 2):
                    last = pe.matmul(bank[2 + b % 2][:, (g - 1) * P:g * P], k.qT[:, g * QPG + qh, d::4],
                                     k.kT[:, g * KVPG + kv, d::4], start=True, stop=True)
                last.then_inc(s.S, 1)

            scores(0)
            scores(1)
            for b in range(NB):
                qh, d = blocks[b]
                kv = qh // 2
                pe.wait_ge(s.prob, b + 1)
                wait(pe, s.PTa, b)
                wait(pe, s.PTb, b)
                for n in range(6):
                    last = pe.transpose(bank[4 + n // 4][:, n % 4 * P:(n % 4 + 1) * P],
                                        k.sc[:, b % 2, n * P:(n + 1) * P], k.ident)
                last.then_inc(s.turned, 1)
                if b + 2 < NB:
                    scores(b + 2)
                pe.wait_ge(s.PTa, b + 1)
                pe.wait_ge(s.PTb, b + 1)
                if b >= 2:
                    pe.wait_ge(s.out, b - 1)
                for n in range(6):
                    v = k.V[:, 0, n] if n < 4 else k.V[:, n - 3, d]
                    last = pe.matmul(bank[6 + b % 2][:, 0:P], v[:, kv * HD:(kv + 1) * HD],
                                     k.PT[:, n * P:(n + 1) * P], start=(n == 0), stop=(n == 5))
                last.then_inc(s.O, 1)

        @block.vector
        def _(dve):
            k.R.arrived(dve, 5)
            k.R.takes[5] += 1

            def softmax(b):
                qh, d = blocks[b]
                sc = k.sc[:, b % 2, :]
                dve.wait_ge(s.S, b + 1)
                if b >= 2:
                    dve.wait_ge(s.turned, b - 1)
                dve.scalar_tensor_tensor(sc[:, 0:SEQ], k.dist[:, 3 - d:3 - d + SEQ], -slope(0, qh),
                                         bank[b % 2][:, :], ALU.mult, ALU.add)
                for g in (1, 2):
                    last = dve.scalar_tensor_tensor(sc[:, SEQ + (g - 1) * P:SEQ + g * P],
                                                    k.dist[:, 3 + SEQ + (g - 1) * P:3 + SEQ + g * P], -slope(g, qh),
                                                    bank[2 + b % 2][:, (g - 1) * P:g * P], ALU.mult, ALU.add)
                    if g == 1:
                        last.then_inc(s.biased, 1)
                last.then_inc(s.biased, 1)
                dve.wait_ge(s.biased, 2 * b + 2)
                dve.tensor_reduce(k.peak[:, b % 2:b % 2 + 1], sc, AX.X, ALU.max, negate=True).then_inc(s.peak, 1)

            def normalise(b):
                dve.wait_ge(s.exp, b + 1)
                dve.reciprocal(k.inv[:, b % 2:b % 2 + 1], k.total[:, b % 2:b % 2 + 1]).then_inc(s.inv, 1)
                dve.wait_ge(s.inv, b + 1)
                dve.tensor_scalar(k.sc[:, b % 2, :], k.sc[:, b % 2, :], k.inv[:, b % 2:b % 2 + 1], None,
                                  ALU.mult).then_inc(s.prob, 1)

            softmax(0)
            softmax(1)
            normalise(0)
            for b in range(NB):
                dve.wait_ge(s.turned, b + 1)
                if b:
                    dve.wait_ge(s.O, b)
                dve.tensor_copy(k.PT[:, SEQ:], bank[5][:, 0:2 * P]).then_inc(s.PTb, 1)
                if b + 1 < NB:
                    normalise(b + 1)
                if b + 2 < NB:
                    softmax(b + 2)

        @block.scalar
        def _(act):
            def exps(b):
                act.wait_ge(s.peak, b + 1)
                sc = k.sc[:, b % 2, :]
                act.activation(sc, sc, ACT.Exp, bias=k.peak[:, b % 2:b % 2 + 1],
                               accum_out=k.total[:, b % 2:b % 2 + 1]).then_inc(s.exp, 1)

            exps(0)
            exps(1)
            for b in range(NB):
                qh, d = blocks[b]
                act.wait_ge(s.turned, b + 1)
                if b:
                    act.wait_ge(s.O, b)
                act.activation(k.PT[:, 0:SEQ], bank[4][:, :], ACT.Copy).then_inc(s.PTa, 1)
                if b + 2 < NB:
                    exps(b + 2)
                act.wait_ge(s.O, b + 1)
                act.activation(k.aoT[:, qh, d::4], bank[6 + b % 2][:, 0:P], ACT.Copy).then_inc(s.out, 1)
            load_sqrt_table(act, k)

        @block.sync
        def _(sp):
            following(sp)




def route(k, layer, following):
    tag = f"rt{layer}"
    s = norm_semaphores(k, tag)
    gain = k.g_ffn[:, layer, :]
    (s.hi, s.res1, s.mid, s.res2, s.lo, s.logits, s.gdiff, s.gexp, s.ediff, s.eexp, s.chosen, s.ranks, s.steps) = (
        k.sem(f"{tag}_{name}") for name in
        ("hi", "res1", "mid", "res2", "lo", "logits", "gdiff", "gexp", "ediff", "eexp", "chosen", "ranks",
         "steps"))
    lg, el, eq = k.lg, k.el, k.eq
    with nc_block(k) as block:

        @block.tensor
        def _(pe):
            norm_tensor(pe, k, s)
            norm_chunk(pe, s, 2)
            norm_chunk(pe, s, 3)
            for c in range(DC):
                norm_chunk(pe, s, c)
                for t in range(NT):
                    last = pe.matmul(k.bank[t][:, 0:MG + EXPERTS], k.xnT[:, c, t * P:(t + 1) * P],
                                     k.w_router[:, layer, c, :], start=(c == 0), stop=(c == DC - 1))
            last.then_inc(s.logits, 1)
            pe.wait_ge(s.chosen, 1)
            for t in range(NT):
                out = k.bank[1][:, t * EXPERTS:(t + 1) * EXPERTS]
                for u in range(t):
                    pe.matmul(out, k.ones_b, k.M[:, u, :], start=(u == 0), stop=False)
                pe.matmul(out, k.before_b, k.M[:, t, :], start=(t == 0), stop=True)
            out = k.bank[1][:, NT * EXPERTS:(NT + 1) * EXPERTS]
            for u in range(NT):
                last = pe.matmul(out, k.ones_b, k.M[:, u, :], start=(u == 0), stop=(u == NT - 1))
            last.then_inc(s.ranks, 1)

        @block.scalar
        def _(act):
            def highest():
                for t in range(NT):
                    act.wait_ge(s.xn_odd if t % 2 else s.xn, t // 2 + 1)
                    act.activation(k.xs[:, 0, t, :], k.xn[:, t, :], ACT.Copy).then_inc(s.hi, 1)

            def lowest(t):
                act.wait_ge(s.res2, t + 1)
                act.activation(k.xs[:, 2, t, :], k.xn[:, t, :], ACT.Copy).then_inc(s.lo, 1)

            norm_scalar(act, k, s, gain, meanwhile=highest)
            for t in range(NT):
                act.wait_ge(s.res1, t + 1)
                act.activation(k.xs[:, 1, t, :], k.xn[:, t, :], ACT.Copy).then_inc(s.mid, 1)
            act.wait_ge(s.gdiff, 1)
            act.activation(k.ge[:, :, :], k.gd[:, :, :], ACT.Exp).then_inc(s.gexp, 1)
            lowest(0)
            lowest(1)
            act.wait_ge(s.ediff, 1)
            act.activation(k.e2[:, :], k.ed[:, :], ACT.Exp).then_inc(s.eexp, 1)
            lowest(2)
            lowest(3)

        @block.gpsimd
        def _(pool):
            pool.wait_ge(s.turned, DC)
            for t in range(NT):
                pool.wait_ge(s.hi, t + 1)
                pool.tensor_tensor(k.xn[:, t, :], k.xn[:, t, :], k.xs[:, 0, t, :], ALU.subtract).then_inc(s.res1, 1)
            for t in range(NT):
                pool.wait_ge(s.mid, t + 1)
                pool.tensor_tensor(k.xn[:, t, :], k.xn[:, t, :], k.xs[:, 1, t, :], ALU.subtract).then_inc(s.res2, 1)

        @block.vector
        def _(dve):
            norm_vector(dve, k, s, gain)
            ch = Chain(dve, s.steps)
            dve.wait_ge(s.logits, 1)
            for t in range(NT):
                logits = dve.tensor_tensor(lg[:, t, :], k.bank[t][:, 0:MG + EXPERTS], k.b_router[:, layer, :], ALU.add)
            ch.link(logits)
            gl = lg[:, :, 0:MG]
            ch.link(dve.tensor_reduce(k.gm[:, :], gl, AX.X, ALU.max))
            dve.tensor_tensor(k.gd[:, :, :], gl, bcast(k.gm[:, :], 2, MG), ALU.subtract).then_inc(s.gdiff, 1)
            ch.link(dve.tensor_tensor(k.gq[:, :, :], gl, bcast(k.gm[:, :], 2, MG), ALU.is_equal))
            ch.link(dve.tensor_tensor(k.gq[:, :, :], k.gq[:, :, :], bcast(k.first[:, 0:MG], 1, NT), ALU.mult))
            ch.link(dve.tensor_reduce(k.gs[:, :], k.gq[:, :, :], AX.X, ALU.max))
            ch.link(dve.tensor_tensor(k.gq[:, :, :], k.gq[:, :, :], bcast(k.gs[:, :], 2, MG), ALU.is_equal))
            ch.link(dve.tensor_scalar(k.gq[:, :, :], k.gq[:, :, :], 1.0, BIG, ALU.subtract, ALU.mult))
            ch.link(dve.tensor_tensor(
                el[:, :, :].rearrange("p t (g e) -> p t g e", g=MG),
                lg[:, :, MG:].rearrange("p t (g e) -> p t g e", g=MG),
                bcast(k.gq[:, :, :], 3, ME), ALU.add))

            def best(m, onehot):
                ch.link(dve.tensor_reduce(m, el[:, :, :], AX.X, ALU.max))
                ch.link(dve.tensor_tensor(eq[:, :, :], el[:, :, :], bcast(m, 2, EXPERTS), ALU.is_equal))
                ch.link(dve.tensor_tensor(eq[:, :, :], eq[:, :, :], bcast(k.first[:, 0:EXPERTS], 1, NT), ALU.mult))
                ch.link(dve.tensor_reduce(k.gs[:, :], eq[:, :, :], AX.X, ALU.max))
                ch.link(dve.tensor_tensor(onehot, eq[:, :, :], bcast(k.gs[:, :], 2, EXPERTS), ALU.is_equal))

            best(k.m1[:, :], k.oh1[:, :, :])
            ch.link(dve.scalar_tensor_tensor(el[:, :, :], k.oh1[:, :, :], -BIG, el[:, :, :], ALU.mult, ALU.add))
            best(k.m2[:, :], k.oh2[:, :, :])
            dve.tensor_tensor(k.ed[:, :], k.m2[:, :], k.m1[:, :], ALU.subtract).then_inc(s.ediff, 1)
            dve.tensor_tensor(k.M[:, :, :], k.oh1[:, :, :], k.oh2[:, :, :], ALU.add).then_inc(s.chosen, 1)
            dve.wait_ge(s.gexp, 1)
            ch.link(dve.tensor_reduce(k.gs[:, :], k.ge[:, :, :], AX.X, ALU.add))
            dve.wait_ge(s.eexp, 1)
            ch.link(dve.scalar_tensor_tensor(k.gs[:, :], k.e2[:, :], 1.0, k.gs[:, :], ALU.add, ALU.mult))
            ch.link(dve.reciprocal(k.c1[:, :], k.gs[:, :]))
            ch.link(dve.tensor_tensor(k.c2[:, :], k.c1[:, :], k.e2[:, :], ALU.mult))
            ch.link(dve.tensor_tensor(k.oh1[:, :, :], k.oh1[:, :, :], bcast(k.c1[:, :], 2, EXPERTS), ALU.mult))
            ch.link(dve.tensor_tensor(k.oh2[:, :, :], k.oh2[:, :, :], bcast(k.c2[:, :], 2, EXPERTS), ALU.mult))
            ch.link(dve.tensor_tensor(k.Wt[:, :, :], k.oh1[:, :, :], k.oh2[:, :, :], ALU.add))
            dve.wait_ge(s.chosen, 1)
            ch.link(dve.tensor_scalar(k.rank[:, :, :], k.M[:, :, :], NOT_CHOSEN, NOT_CHOSEN, ALU.mult, ALU.subtract))
            dve.wait_ge(s.ranks, 1)
            raw = k.bank[1][:, 0:NT * EXPERTS].rearrange("p (t e) -> p t e", t=NT)
            ch.link(dve.tensor_tensor(k.rank[:, :, :], k.rank[:, :, :], raw, ALU.add))
            total = k.bank[1][:, NT * EXPERTS:(NT + 1) * EXPERTS]
            ch.link(dve.tensor_reduce(k.most[:, :], total, AX.X, ALU.max))
            ch.link(dve.tensor_scalar(k.most_i[:, :], k.most[:, :], 1.0, None, ALU.subtract))
            dve.tensor_scalar(k.extra[:, layer:layer + 1], k.most_i[:, :], SLOTS.bit_length() - 1,
                              None, ALU.logical_shift_right).then_inc(s.steps, 1)

        @block.sync
        def _(sp):
            following(sp)


def expert_semaphores(k, tag):
    s = Net()
    (s.half0, s.half2, s.half4, s.slots, s.weighted, s.shift, s.gathered, s.xT, s.h1, s.h3, s.silu, s.hidden,
     s.hidden_turned, s.hT, s.S_turned, s.S, s.yps, s.y, s.spread, s.added,
     s.Sb, s.hi, s.rest, s.mid, s.low) = (
         k.sem(f"{tag}_{name}") for name in
         ("half0", "half2", "half4", "slots", "weighted", "shift", "gathered", "xT", "h1", "h3", "silu",
          "hidden", "hidden_turned", "hT", "S_turned", "S", "yps", "y", "spread", "added", "Sb", "hi", "rest", "mid",
          "low"))
    return s


def build_slots(dve, k, s, pair, i, reuse):
    if reuse:
        wait(dve, s.gathered, 2 * i)
        wait(dve, s.weighted, i)
    ranks = k.rank[:, :, bass.ds(pair * 2, 2)]
    if not (isinstance(i, int) and i == 0):
        wait(dve, s.shift, i)
    dve.tensor_tensor(
        k.slot1h[:, :, :].rearrange("p t (e n) -> p t e n", e=2), bcast(ranks, 3, SLOTS),
        bcast(bcast(k.iota[:, 0:SLOTS], 1, 2), 1, NT), ALU.is_equal).then_inc(s.slots, 1)
    wait(dve, s.slots, i + 1)
    dve.tensor_scalar(ranks, ranks, float(SLOTS), None, ALU.subtract).then_inc(s.shift, 1)


def weigh_slots(dve, k, s, pair, i):
    wait(dve, s.S_turned, i)
    wait(dve, s.slots, i + 1)
    dve.tensor_tensor(
        k.slotw[:, :, :].rearrange("p t (e n) -> p t e n", e=2),
        k.slot1h[:, :, :].rearrange("p t (e n) -> p t e n", e=2),
        bcast(k.Wt[:, :, bass.ds(pair * 2, 2)], 3, SLOTS), ALU.mult).then_inc(s.weighted, 1)


def evacuate_gather(dve, k, s, layer, i):
    for half in range(2):
        wait(dve, s.gathered, 2 * i + half + 1)
        gain = k.g_ffn[:, layer, 4 * half:4 * half + 4]
        dve.tensor_tensor(k.xT[:, 4 * half:4 * half + 4, :],
                          k.bank[6 + half][:, :].rearrange("p (c n) -> p c n", c=4),
                          bcast(gain, 2, P), ALU.mult).then_inc(s.xT, 1)


def hidden(dve, k, s, i):
    dve.wait_ge(s.silu, i + 1)
    dve.wait_ge(s.h3, i + 1)
    dve.tensor_tensor(k.h[:, :], k.h1s[:, :], k.bank[1][:, :], ALU.mult).then_inc(s.hidden, 1)


def halves_of(k, n):
    return k.y[:, n * HALF:(n + 1) * HALF], [k.yp[:, part, n * HALF:(n + 1) * HALF] for part in range(3)]


def add_results(dve, k, s, i):
    wait(dve, s.spread, 8 * i)
    dve.wait_ge(s.S, i + 1)
    dve.tensor_scalar(k.Sb[:, :], k.S[:, :], 0.0, None, ALU.not_equal).then_inc(s.Sb, 1)

    def rest(n):
        y, parts = halves_of(k, n)
        dve.wait_ge(s.hi, 2 * i + n + 1)
        dve.tensor_tensor(y, y, parts[0], ALU.subtract).then_inc(s.rest, 1)

    def low(n):
        y, parts = halves_of(k, n)
        dve.wait_ge(s.mid, 2 * i + n + 1)
        dve.tensor_tensor(parts[2], y, parts[1], ALU.subtract).then_inc(s.low, 1)

    def add(j):
        n, t = j // NT, j % NT
        dve.wait_ge(s.spread, 8 * i + j + 1)
        out = k.H[:, t, n * HALF:(n + 1) * HALF]
        dve.tensor_tensor(out, out, k.bank[6 + j % 2][:, :], ALU.add).then_inc(s.added, 1)

    rest(0)
    low(0)
    add(0)
    rest(1)
    add(1)
    low(1)
    for j in range(2, 2 * NT):
        add(j)


def gather(pe, k, s, i, after):
    pe.wait_ge(s.slots, i + 1)
    wait(pe, s.added, after)
    for half in range(2):
        for c in range(4 * half, 4 * half + 4):
            n = 0
            for part in range(3):
                for t in range(NT):
                    last = pe.matmul(k.bank[6 + half][:, (c % 4) * P:(c % 4 + 1) * P], k.xs[:, part, t, c::DC],
                                     k.slot1h[:, t, :], start=(n == 0), stop=(n == 3 * NT - 1))
                    n += 1
        last.then_inc(s.gathered, 1)


def expert_matmuls(pe, k, arrived, m, x, chunks, out, cols, half, done):
    per = chunks // 2
    for c in range(chunks):
        slot = 2 * m + c // per
        if arrived and c % per == 0:
            arrived(slot)
        w = k.ring[:, slot, :].rearrange("p (e c n) -> p e c n", e=2, c=per)
        for e in range(2):
            last = pe.matmul(out[e * SLOTS:(e + 1) * SLOTS, :], x[:, c, e * SLOTS:(e + 1) * SLOTS],
                             w[:, e, c % per, cols], start=(c == 0), stop=(c == chunks - 1))
        if half and c == per - 1:
            last.then_inc(half, 1)
    last.then_inc(done, 1)


def expert_up(pe, k, s, i, arrived):
    pe.wait_ge(s.xT, 2 * i + 2)
    wait(pe, s.S, i)
    expert_matmuls(pe, k, arrived, 0, k.xT, DC, k.bank[0], slice(0, FF), s.half0, s.h1)
    expert_matmuls(pe, k, arrived, 1, k.xT, DC, k.bank[1], slice(0, FF), s.half2, s.h3)


def expert_turn(pe, k, s, i):
    pe.wait_ge(s.hidden, i + 1)
    for c in range(FC):
        last = pe.transpose(k.bank[4][:, c * P:(c + 1) * P], k.h[:, c::FC], k.ident)
    last.then_inc(s.hidden_turned, 1)
    pe.wait_ge(s.weighted, i + 1)
    for t in range(NT):
        last = pe.transpose(k.bank[0][:, t * P:(t + 1) * P], k.slotw[:, t, :], k.ident)
    last.then_inc(s.S_turned, 1)


def expert_down(pe, k, s, i, arrived):
    pe.wait_ge(s.hT, i + 1)
    for n in range(2):
        expert_matmuls(pe, k, None if n else arrived, 2, k.hT, FC, k.bank[2 + n],
                       slice(n * HALF, (n + 1) * HALF), s.half4 if n else None, s.yps)


def spread(pe, k, s, i, evacuated):
    pe.wait_ge(s.Sb, i + 1)
    pe.wait_ge(s.xT, evacuated)
    for n in range(2):
        pe.wait_ge(s.low, 2 * i + n + 1)
        _, parts = halves_of(k, n)
        for t in range(NT):
            j = n * NT + t
            if j >= 2:
                pe.wait_ge(s.added, 8 * i + j - 1)
            for m in range(3):
                last = pe.matmul(k.bank[6 + j % 2][:, :], k.Sb[:, t * P:(t + 1) * P], parts[m], start=(m == 0),
                                 stop=(m == 2))
            last.then_inc(s.spread, 1)


def expert_scalar(act, k, s, i, alone=False):
    before = (lambda sem, value: None) if alone else (lambda sem, value: wait(act, sem, value))
    act.wait_ge(s.h1, i + 1)
    wait(act, s.hidden, i)
    act.activation(k.h1s[:, :], k.bank[0][:, :], ACT.Silu).then_inc(s.silu, 1)
    act.wait_ge(s.hidden_turned, i + 1)
    act.activation(k.hT[:, :, :], k.bank[4][:, :].rearrange("p (c n) -> p c n", c=FC), ACT.Copy).then_inc(s.hT, 1)
    act.wait_ge(s.S_turned, i + 1)
    before(s.Sb, i)
    before(s.y, 2 * i)
    act.activation(k.S[:, :], k.bank[0][:, :], ACT.Copy, accum_out=k.slot_weight[:, :]).then_inc(s.S, 1)
    act.wait_ge(s.S, i + 1)
    for n in range(2):
        y, parts = halves_of(k, n)
        act.wait_ge(s.yps, 2 * i + n + 1)
        before(s.low, 2 * i + n - 1)
        act.activation(y, k.bank[2 + n][:, :], ACT.Copy, scale=k.slot_weight[:, 0:1]).then_inc(s.y, 1)
        act.wait_ge(s.y, 2 * i + n + 1)
        before(s.spread, 8 * i + 4 * n - 4)
        act.activation(parts[0], y, ACT.Copy).then_inc(s.hi, 1)
        act.wait_ge(s.rest, 2 * i + n + 1)
        act.activation(parts[1], y, ACT.Copy).then_inc(s.mid, 1)


def experts(k, layer, following):
    s = expert_semaphores(k, f"mx{layer}")
    R = k.R
    frees = ((s.half0, 1), (s.h1, 1), (s.half2, 1), (s.h3, 1), (s.half4, 1), (s.yps, 2))
    with nc_block(k) as block:

        @block.tensor
        def _(pe):
            def pair(i, last=False):
                def arrived(slot):
                    R.arrived(pe, slot, i)

                expert_up(pe, k, s, i, arrived)
                if not last:
                    gather(pe, k, s, i + 1, 8 * i)
                expert_turn(pe, k, s, i)
                expert_down(pe, k, s, i, arrived)
                spread(pe, k, s, i, 2 * i + (2 if last else 4))

            gather(pe, k, s, 0, 0)
            pair(0)
            with pe.Fori(1, PAIRS - 1) as i:
                pair(i)
            pair(PAIRS - 1, last=True)
            for slot in range(RING):
                R.takes[slot] += PAIRS
                R.free[slot] = (frees[slot][0], PAIRS * frees[slot][1])

        @block.vector
        def _(dve):
            def pair(i, last=False):
                weigh_slots(dve, k, s, i, i)
                if not last:
                    build_slots(dve, k, s, i + 1, i + 1, True)
                hidden(dve, k, s, i)
                if not last:
                    evacuate_gather(dve, k, s, layer, i + 1)
                add_results(dve, k, s, i)

            build_slots(dve, k, s, 0, 0, False)
            evacuate_gather(dve, k, s, layer, 0)
            pair(0)
            with dve.Fori(1, PAIRS - 1) as i:
                pair(i)
            pair(PAIRS - 1, last=True)

        @block.scalar
        def _(act):
            expert_scalar(act, k, s, 0)
            with act.Fori(1, PAIRS) as i:
                expert_scalar(act, k, s, i)
            load_sqrt_table(act, k)

        @block.sync
        def _(sp):
            with sp.Fori(1, PAIRS) as i:
                def load(slot, dst, src):
                    sem, per = frees[slot]
                    sp.wait_ge(sem, i * per)
                    sp.dma_start(dst, src).then_inc(R.landed[slot], 16)

                load_expert_pair(k, layer, i, load)
            extra = sp.value_load(k.extra[0:1, layer:layer + 1], min_val=0, max_val=SEQ // SLOTS - 1)
            with sp.If(extra < 1):
                following(sp)


def more_experts(k, layer, following):
    s = expert_semaphores(k, f"my{layer}")
    landed, done = k.sem(f"my{layer}_landed"), k.sem(f"my{layer}_done")

    def loop(eng, body):
        extra = eng.value_load(k.extra[0:1, layer:layer + 1], min_val=0, max_val=SEQ // SLOTS - 1)
        with eng.If(extra > 0):
            with eng.Fori(0, extra) as p:
                with eng.Fori(0, PAIRS) as pair:
                    i = p * PAIRS + pair
                    eng.wait_ge(done, i + 1)
                    body(i, pair)

    with nc_block(k) as block:

        @block.tensor
        def _(pe):
            def step(i, pair):
                def arrived(slot):
                    pe.wait_ge(landed, (i + 1) * (16 * RING))

                gather(pe, k, s, i, 0)
                expert_up(pe, k, s, i, arrived)
                expert_turn(pe, k, s, i)
                expert_down(pe, k, s, i, arrived)
                spread(pe, k, s, i, 2 * i + 2)

            loop(pe, step)

        @block.vector
        def _(dve):
            dve.sem_inc(done, 1)

            def step(i, pair):
                build_slots(dve, k, s, pair, i, True)
                weigh_slots(dve, k, s, pair, i)
                evacuate_gather(dve, k, s, layer, i)
                hidden(dve, k, s, i)
                add_results(dve, k, s, i)
                dve.wait_ge(s.added, 8 * i + 8)
                dve.sem_inc(done, 1)

            loop(dve, step)

        @block.scalar
        def _(act):
            loop(act, lambda i, pair: expert_scalar(act, k, s, i, alone=True))

        @block.sync
        def _(sp):
            def load(slot, dst, src):
                sp.dma_start(dst, src).then_inc(landed, 16)

            loop(sp, lambda i, pair: load_expert_pair(k, layer, pair, load))
            extra = sp.value_load(k.extra[0:1, layer:layer + 1], min_val=0, max_val=SEQ // SLOTS - 1)
            with sp.If(extra > 0):
                sp.wait_ge(done, extra * PAIRS + 1)
                following(sp)




def embed(k, layer, following, store=False):
    tag = f"pe{layer}"
    s = norm_semaphores(k, tag)
    (s.gate, s.sig, s.prod, s.sum, s.p) = (
        k.sem(f"{tag}_{name}") for name in
        ("gate", "sig", "prod", "sum", "p"))
    R = k.R
    gain = k.g_ple[:, layer, :]
    with nc_block(k) as block:

        @block.tensor
        def _(pe):
            wp = R.flat(2, 2048).rearrange("p (c n) -> p c n", c=2)

            def from_p(j):
                n, t = j // NT, j % NT
                for c in range(2):
                    last = pe.matmul(k.bank[4 + j % 4][:, :], k.pT[:, c, t * P:(t + 1) * P],
                                     wp[:, c, n * HALF:(n + 1) * HALF], start=(c == 0), stop=(c == 1))
                return last

            R.arrived(pe, 2)
            pe.wait_ge(s.p, 16)
            from_p(0)
            from_p(1)
            norm_tensor(pe, k, s, chunks=range(4), banks=4)
            from_p(2)
            norm_tensor(pe, k, s, chunks=range(4, DC), banks=4)
            from_p(3)
            norm_chunk(pe, s, DC - 2)
            norm_chunk(pe, s, DC - 1)
            for n in range(2):
                R.arrived(pe, n)
                w = R.flat(n).rearrange("p (c n) -> p c n", c=DC)
                for t in range(NT):
                    j = n * NT + t
                    if j >= 4:
                        pe.wait_ge(s.prod, j - 3)
                    for c in range(DC):
                        last = pe.matmul(k.bank[j % 4][:, :], k.xnT[:, c, t * P:(t + 1) * P], w[:, c, :],
                                         start=(c == 0), stop=(c == DC - 1))
                    if j >= 4:
                        last = from_p(j)
                    last.then_inc(s.gate, 1)
                R.taken(n, s.gate, (n + 1) * NT)
            R.taken(2, s.gate, 2 * NT)

        @block.scalar
        def _(act):
            norm_scalar(act, k, s, gain, banks=4)
            for j in range(2 * NT):
                act.wait_ge(s.gate, j + 1)
                if j >= 2:
                    act.wait_ge(s.sum, j - 1)
                act.activation(k.sg[:, j % 2, :], k.bank[j % 4][:, :], ACT.Sigmoid).then_inc(s.sig, 1)
            if not store:
                load_sqrt_table(act, k)

        @block.vector
        def _(dve):
            norm_vector(dve, k, s, gain, banks=4)
            for j in range(2 * NT):
                n, t = j // NT, j % NT
                dve.wait_ge(s.sig, j + 1)
                dve.tensor_tensor(k.sg[:, j % 2, :], k.sg[:, j % 2, :], k.bank[4 + j % 4][:, :],
                                  ALU.mult).then_inc(s.prod, 1)
                dve.wait_ge(s.prod, j + 1)
                out = k.H[:, t, n * HALF:(n + 1) * HALF]
                dve.tensor_tensor(out, out, k.sg[:, j % 2, :], ALU.add).then_inc(s.sum, 1)

        @block.sync
        def _(sp):
            sp.dma_start(k.pT[:, :, :], k.p_t[layer].rearrange("(p c) n -> p c n", c=2)).then_inc(s.p, 16)
            if store:
                for t in range(NT):
                    sp.wait_ge(s.sum, NT + t + 1)
                    sp.dma_start(k.out_t[:, t, :], k.H[:, t, :]).then_inc(k.s_out, 16)
                sp.wait_ge(k.s_out, 16 * NT)
            following(sp)


def nc_block(k):
    return k.nc.Block()


def host_distances():
    j = np.arange(P)
    dist = (4 * j[:, None] - np.arange(-3, SEQ)[None, :]).astype(np.float32)
    parts = [np.where((dist >= 0) & (dist <= WINDOW), dist, BIG)]
    steps = j[:, None] - j[None, :]
    for every in (1, 4):
        parts.append(np.where((steps >= 0) & (steps % every == 0), 4.0 * steps, BIG))
    return np.concatenate(parts, axis=1).astype(np.float32)


CONSTS = (("ident", P), ("ones", P), ("before", P), ("upto", P), ("iota", P),
          ("first", EXPERTS), ("eps", 1))


def host_constants():
    i = np.arange(P)
    t = {
        "ident": np.eye(P),
        "ones": np.ones((P, P)),
        "before": (i[:, None] < i[None, :]),
        "upto": (i[:, None] <= i[None, :]),
        "eps": np.full((P, 1), EPS),
        "iota": np.broadcast_to(i[None, :], (P, P)),
        "first": np.broadcast_to(EXPERTS - np.arange(EXPERTS)[None, :], (P, EXPERTS)),
    }
    return np.concatenate([np.asarray(t[n], np.float32) for n, _ in CONSTS], axis=1)


def host_join():
    i = np.arange(P)
    return np.ascontiguousarray(np.stack(
        [((i[:, None] >> l) % 2 == 1) & ((i[:, None] >> l) == (i[None, :] >> l) + 1) for l in range(LEVELS)],
        axis=1).astype(np.float32))


def build(nc, t, out):
    with ExitStack() as ctx:
        k = Net()
        k.nc = nc
        scope = [ctx]

        def sb(name, shape, dt=F32):
            names.append(name)
            return scope[-1].enter_context(nc.sbuf_tensor(f"{name}_{len(names)}", shape, dt))

        names = []
        k.sems = []

        def sem(name):
            k.sems.append(nc.alloc_semaphore(name=name))
            return k.sems[-1]

        k.sem = sem
        k.bank = [ctx.enter_context(nc.psum_tensor(f"bank{i}", [P, HALF], F32)) for i in range(8)]
        k.w1, k.w3, k.w2, k.w_heads, k.p_t = (t[name] for name in ("w1", "w3", "w2", "w_heads", "p_t"))
        k.w_gate, k.w_proj = t["w_ple_gate"], t["w_ple_proj"]
        k.out_t = out[0].rearrange("(t p) d -> p t d", p=P)

        k.ring = sb("ring", [P, RING, 4096])
        k.H = sb("H", [P, NT, D])
        k.xnT = sb("xnT", [P, DC, SEQ])
        k.consts = sb("consts", [P, sum(n for _, n in CONSTS)])
        k.consts_b = sb("consts_b", [P, 2, P], BF16)
        ends = np.cumsum([n for _, n in CONSTS])
        k.ident, k.ones, k.before, k.upto, k.iota, k.first, k.eps = (
            k.consts[:, int(end) - n:int(end)] for (_, n), end in zip(CONSTS, ends))
        k.ones_b, k.before_b = k.consts_b[:, 0, :], k.consts_b[:, 1, :]
        k.g_a = sb("g_a", [P, DC])
        k.g_o = sb("g_o", [P, 1])
        k.scrap = sb("scrap", [P, 1])
        k.g_kv = sb("g_kv", [P, DC])
        k.g_b = sb("g_b", [P, DC])
        k.g_kq = sb("g_kq", [P, 2, GROUPS])
        k.g_ffn = sb("g_ffn", [P, 2, DC])
        k.g_ple = sb("g_ple", [P, 2, DC])
        (k.ss, k.var, k.std, k.rstd) = (
            sb(name, [P, NT]) for name in
            ("ss", "var", "std", "rstd"))
        k.w_router = sb("w_router", [P, 2, DC, MG + EXPERTS])
        k.b_router = sb("b_router", [P, 2, MG + EXPERTS])
        k.extra = sb("extra", [P, 2], I32)
        k.s_out = k.sem("stored")
        k.R = Ring(k.ring, [k.sem(f"landed{i}") for i in range(RING)])
        kept = len(k.sems)

        def end_phase():
            nc.clear_and_free_semaphores(k.sems[kept:])
            nc.all_engine_barrier()
            del k.sems[kept:]
            k.R.free = [None] * RING

        def phase():
            st = ExitStack()
            scope.append(st)
            st.callback(scope.pop)
            return st

        with phase():
            (k.beta, k.glog, k.G, k.eG, k.eGlast, k.eGrest, k.beG, k.ax, k.sp) = (
                sb(name, [P, NT, HEADS]) for name in
                ("beta", "glog", "G", "eG", "eGlast", "eGrest", "beG", "ax", "sp"))
            k.eA = sb("eA", [P, HEADS])
            k.dt_bias = sb("dt_bias", [P, HEADS])
            k.w_ab = sb("w_ab", [P, DC, 2 * HEADS])
            k.conv_w = sb("conv_w", [P, 3, HEADS * CONV])
            k.join = sb("join", [P, LEVELS, P])

            early = [
                (k.consts[:, :], t["consts"]),
                (k.g_a[:, :], t["a_norm"][0].rearrange("(p c) -> p c", c=DC)),
                (k.w_ab[:, :, :], t["w_ab"].rearrange("(p c) n -> p c n", c=DC)),
                (k.eA[:, :], t["a_A_log"][0:1, :].to_broadcast([P, HEADS])),
                (k.dt_bias[:, :], t["a_dt_bias"][0:1, :].to_broadcast([P, HEADS])),
            ]
            late = [
                (k.conv_w[:, :, :], t["conv_w"]),
                (k.join[:, :, :], t["join"]),
                (k.g_o[:, :], t["a_o_norm"][0].rearrange("(p c) -> p c", c=1)),
                (k.g_kv[:, :], t["kv_norm"].rearrange("(p c) -> p c", c=DC)),
                (k.g_b[:, :], t["b_norm"][0].rearrange("(p c) -> p c", c=DC)),
                (k.g_kq[:, :, :], t["g_kq"]),
                (k.g_ffn[:, :, :], t["ffn_norm"].rearrange("l (p c) -> p l c", c=DC)),
                (k.g_ple[:, :, :], t["ple_norm"].rearrange("l (p c) -> p l c", c=DC)),
            ]
            for l in range(2):
                late += [(k.w_router[:, l, :, :], t["w_router"][l].rearrange("(p c) n -> p c n", c=DC)),
                         (k.b_router[:, l, :], t["b_router"][l:l + 1, :].to_broadcast([P, MG + EXPERTS]))]
            k.n_early, k.n_late = 16 * len(early), 16 * len(late)

            def loads(sp, g):
                x = t["x"][0].rearrange("(t p) d -> p t d", p=P)
                for n in range(NT):
                    sp.dma_start(k.H[:, n, :], x[:, n, :]).then_inc(g.x[n], 16)
                for dst, src in early:
                    sp.dma_start(dst, src).then_inc(g.early, 16)
                for h in range(2):
                    dst, src = load_head(k, h, h)
                    sp.dma_start(dst, src).then_inc(k.R.landed[h], 16)
                for dst, src in late:
                    sp.dma_start(dst, src).then_inc(g.late, 16)
                w_out = t["a_w_out"][0].rearrange("(h p) n -> p h n", p=P)
                for n in range(2):
                    sp.dma_start(k.R.flat(2 + n).rearrange("p (h n) -> p h n", h=HEADS),
                                 w_out[:, :, n * HALF:(n + 1) * HALF]).then_inc(k.R.landed[2 + n], 16)

            k.oT = k.R.flat(4).rearrange("p (h n) -> p h n", h=HEADS)
            k.qkvz = k.R.flat(5).rearrange("p (b j n) -> p b j n", b=2, j=4)
            k.cv = sb("cv", [P, 3, SEQ])
            k.sqr = sb("sqr", [P, 2, SEQ])
            k.rnorm = sb("rnorm", [P, 3, SEQ])
            (k.glogB, k.dif, k.lo, k.hi, k.kb, k.kd, k.vb, k.T, k.V, k.A, k.us) = (
                sb(name, [P, NT, P]) for name in
                ("glogB", "dif", "lo", "hi", "kb", "kd", "vb", "T", "V", "A", "us"))
            (k.qg, k.eGrow, k.nWT, k.osq, k.og) = (
                sb(name, [P, SEQ]) for name in
                ("qg", "eGrow", "nWT", "osq", "og"))
            k.state = sb("state", [P, 2, P])
            shared = sb("shared", [P, NT * D])
            k.xn = shared[:, :].rearrange("p (t d) -> p t d", t=NT)
            k.C = shared[:, 0:LEVELS * SEQ].rearrange("p (l t n) -> p l t n", l=LEVELS, t=NT)
            k.X = shared[:, LEVELS * SEQ:].rearrange("p (t n) -> p t n", t=NT)
            delta(k, loads, lambda sp: prefetch_experts(sp, k, 0))
            end_phase()

        def load_kv(sp):
            for w, slot in ((t["w_kv"], 3), (t["b_w_q"][0], 0)):
                for g in range(GROUPS):
                    k.R.load(sp, slot + g, k.R.flat(slot + g).rearrange("p (c n) -> p c n", c=DC),
                             w.rearrange("(p c) n -> p c n", c=DC)[:, :, g * HALF:(g + 1) * HALF])

        for layer in range(2):
            with phase():
                k.xn = sb("xn", [P, NT, D])
                k.xs = sb("xs", [P, 3, NT, D], BF16)
                k.lg = sb("lg", [P, NT, MG + EXPERTS])
                (k.gd, k.gq, k.ge) = (
                    sb(name, [P, NT, MG]) for name in
                    ("gd", "gq", "ge"))
                (k.gm, k.gs, k.m1, k.m2, k.ed, k.e2, k.c1, k.c2) = (
                    sb(name, [P, NT]) for name in
                    ("gm", "gs", "m1", "m2", "ed", "e2", "c1", "c2"))
                (k.el, k.eq, k.oh1, k.oh2, k.Wt, k.rank) = (
                    sb(name, [P, NT, EXPERTS]) for name in
                    ("el", "eq", "oh1", "oh2", "Wt", "rank"))
                k.M = sb("M", [P, NT, EXPERTS], BF16)
                k.most = sb("most", [P, 1])
                k.most_i = sb("most_i", [P, 1], I32)
                k.slot1h = sb("slot1h", [P, NT, 2 * SLOTS], BF16)
                k.slotw = sb("slotw", [P, NT, 2 * SLOTS])
                k.xT = sb("xT", [P, DC, 2 * SLOTS])
                k.h1s = sb("h1s", [P, FF])
                k.h = sb("h", [P, FF])
                k.hT = sb("hT", [P, FC, 2 * SLOTS])
                k.S = sb("S", [P, SEQ])
                k.y = sb("y", [P, D])
                k.Sb = sb("Sb", [P, SEQ], BF16)
                k.slot_weight = sb("slot_weight", [P, 1])
                k.yp = sb("yp", [P, 3, D], BF16)
                route(k, layer, lambda sp: None)
                experts(k, layer, lambda sp: prefetch_ple(sp, k, layer))
                more_experts(k, layer, lambda sp: prefetch_ple(sp, k, layer))
            end_phase()
            with phase():
                k.xn = sb("xn", [P, NT, D])
                k.sg = sb("sg", [P, 2, HALF])
                k.pT = sb("pT", [P, 2, SEQ])
                embed(k, layer, load_kv if layer == 0 else (lambda sp: None), store=(layer == 1))
            end_phase()
            if layer == 1:
                break
            with phase():
                k.kT = sb("kT", [P, GROUPS * KVPG, SEQ])
                k.V = sb("V", [P, GROUPS, NT, KVPG * HD])
                k.qT = sb("qT", [P, GROUPS * QPG, SEQ])
                with phase():
                    k.xn = sb("xn", [P, NT, D])
                    k.sqr = sb("sqr", [P, 2, SEQ])
                    k.rnorm = sb("rnorm", [P, 2, SEQ])

                    def weights(slot, per):
                        def of(pe, j):
                            if j % per == 0:
                                k.R.arrived(pe, slot + j // per)
                            return k.R.flat(slot + j // per).rearrange("p (c n) -> p c n", c=DC)[
                                :, :, j % per * HD:(j % per + 1) * HD]
                        return of

                    def after_kv(sp):
                        k.R.load(sp, 3, k.R.flat(3).rearrange("p (h n) -> p h n", h=QPG),
                                 t["b_w_out"][0].rearrange("(h p) n -> p h n", p=P))
                        k.R.load(sp, 5, k.R.flat(5, NDIST), t["dist"])
                        prefetch_experts(sp, k, 1, (4,))

                    head_features(k, "kf", k.g_kv, weights(3, KVPG), GROUPS * KVPG, k.kT, k.g_kq[:, 0, :],
                                  (3, 4, 5), after_kv, values=Values(k))
                    end_phase()
                    head_features(k, "qf", k.g_b, weights(0, QPG), GROUPS * QPG, k.qT, k.g_kq[:, 1, :],
                                  (0, 1, 2), lambda sp: prefetch_experts(sp, k, 1, (0, 1, 2)), scale=HD ** -0.5,
                                  fresh=False)
                    end_phase()
                with phase():
                    k.dist = k.R.flat(5, NDIST)
                    k.sc = sb("sc", [P, 2, NSCORE])
                    k.PT = sb("PT", [P, NSCORE])
                    k.aoT = k.xnT[:, 0:QPG, :]
                    (k.peak, k.total, k.inv) = (
                        sb(name, [P, 2]) for name in
                        ("peak", "total", "inv"))
                    attend(k, lambda sp: None)
                    end_phase()

                    def whole(pe, n):
                        if n == 0:
                            k.R.arrived(pe, 3)
                        w = k.R.flat(3).rearrange("p (h n) -> p h n", h=QPG)
                        return lambda c: w[:, c, n * HALF:(n + 1) * HALF]

                    def then(sp, done):
                        k.R.takes[3] += 1
                        k.R.free[3] = (done, 2 * NT)
                        prefetch_experts(sp, k, 1, (5,))
                        prefetch_experts(sp, k, 1, (3,))

                    project_out(k, "at_out", k.aoT, QPG, whole, then)
                    end_phase()


_INS = ["x", "kv_norm", "w_kv", "b_norm", "b_w_q", "b_w_out", "a_norm", "a_A_log", "a_dt_bias", "a_o_norm",
        "a_w_out", "ffn_norm", "w1", "w3", "w2", "ple_norm", "w_ple_gate", "w_ple_proj"]


def kernel(**inputs):
    import numpy as _np
    import concourse.bacc as _bacc
    from concourse import mybir as _mybir
    from concourse.bass_utils import run_bass_kernel_spmd as _run

    nc = _bacc.Bacc("TRN2", target_bir_lowering=False, num_devices=1)
    data = {name: _np.ascontiguousarray(inputs[name]) for name in _INS}
    data["p_t"] = _np.ascontiguousarray(_np.asarray(inputs["p"])[:, 0].transpose(0, 2, 1))
    w_in = _np.asarray(inputs["a_w_in"])[0]
    heads = w_in[:, :4 * HEADS * DK].reshape(P, DC, 4, HEADS, DK)
    data["w_heads"] = _np.ascontiguousarray(heads.transpose(3, 0, 1, 2, 4)).reshape(HEADS, P, 4096)
    data["w_ab"] = _np.ascontiguousarray(w_in[:, 4 * HEADS * DK:])
    taps = _np.asarray(inputs["a_conv"])[0].reshape(CONV, 3, HEADS, P)
    data["conv_w"] = _np.ascontiguousarray(taps.transpose(3, 1, 2, 0)).reshape(P, 3, HEADS * CONV)
    for what in ("w", "b"):
        data[f"{what}_router"] = _np.concatenate(
            [_np.asarray(inputs[f"{what}_router_{part}"]) for part in ("group", "expert")], axis=-1)
    data["g_kq"] = _np.ascontiguousarray(
        _np.stack([_np.asarray(inputs["k_norm"]), _np.asarray(inputs["b_q_norm"])[0]]).transpose(2, 0, 1))
    data["dist"] = host_distances()
    data["consts"] = host_constants()
    data["join"] = host_join()
    arrays, aps = {}, {}
    for name, a in data.items():
        arrays[f"in_{name}"] = a
        aps[name] = nc.dram_tensor(f"in_{name}", a.shape, _mybir.dt.from_np(a.dtype), kind="ExternalInput").ap()
    out = nc.dram_tensor("out_0", (1, SEQ, D), F32, kind="ExternalOutput").ap()
    build(nc, aps, out)
    r = _run(nc, [arrays], core_ids=[0])
    return r.results[0]["out_0"]
```
